# Optimizing a Trainium2 kernel written in Bass

```python
import jax, jax.numpy as jnp
from jax import lax
import numpy as np

D_MODEL = 1024
BATCH = 1
SEQ = 512
DEPTH = 1

CHUNK = 64
CONV_CH = D_MODEL
CONV_WIDTH = 31
SG_WIDTH = D_MODEL
SG_HEADS = 8
SG_HEAD_DIM = SG_WIDTH // SG_HEADS
SG_BLOCK = 128
N_GROUPS = 4
EXPERTS_PER_GROUP = 8
N_EXPERTS = N_GROUPS * EXPERTS_PER_GROUP
TOP_K = 2
D_EXPERT = D_MODEL // 2
EXPERT_BLOCK = 256
IN_COLS = 2 * CONV_CH + 2 * SG_WIDTH + 2 * D_MODEL
EPS = 1e-6


def rms_norm(x, g):
    xf = x.astype(jnp.float32)
    y = xf * lax.rsqrt(jnp.mean(xf * xf, axis=-1, keepdims=True) + EPS)
    return (y * g.astype(jnp.float32)).astype(x.dtype)

def layer_norm(x, g, b):
    xf = x.astype(jnp.float32)
    mu = jnp.mean(xf, axis=-1, keepdims=True)
    var = jnp.mean(jnp.square(xf - mu), axis=-1, keepdims=True)
    y = (xf - mu) * lax.rsqrt(var + EPS)
    return (y * g.astype(jnp.float32) + b.astype(jnp.float32)).astype(x.dtype)

def conformer_conv_branch(a, conv_w, conv_b, ln_g, ln_b, w_o, b_o):
    a1, a2 = jnp.split(a, 2, axis=-1)
    a = a1 * jax.nn.sigmoid(a2)
    kern = conv_w[:, None, :]
    y = lax.conv_general_dilated(
        a, kern, window_strides=(1,), padding=[(CONV_WIDTH - 1, 0)],
        dimension_numbers=("NWC", "WIO", "NWC"), feature_group_count=CONV_CH) + conv_b
    y = jax.nn.silu(layer_norm(y, ln_g, ln_b))
    return y @ w_o + b_o

def spatial_gating_branch(z, ln_g, ln_b, w_s, b_s, w_o, b_o):
    z = jax.nn.gelu(z, approximate=False)
    u, v = jnp.split(z, 2, axis=-1)
    v = layer_norm(v, ln_g, ln_b)
    bsz, seq, _ = v.shape
    n_blk = seq // SG_BLOCK
    v = v.reshape(bsz, n_blk, SG_BLOCK, SG_HEADS, SG_HEAD_DIM)
    blk = np.arange(SG_BLOCK) // CHUNK
    mask = jnp.asarray(blk[:, None] >= blk[None, :])
    w = w_s * mask[None].astype(w_s.dtype)
    sv = jnp.einsum("hqk,bnkhc->bnqhc", w, v) + b_s.T[:, :, None]
    s = u * sv.reshape(bsz, seq, SG_WIDTH)
    return s @ w_o + b_o

def hierarchical_moe(h, w_rg, b_rg, w_re, b_re, w_gate, w_up, w_down):
    bsz, seq, d = h.shape
    n_tok = bsz * seq
    xt = h.reshape(n_tok, d)
    g_logits = (xt @ w_rg + b_rg).astype(jnp.float32)
    g_prob = jax.nn.softmax(g_logits, axis=-1)
    g_sel = jnp.argmax(g_logits, axis=-1)
    g_w = jnp.take_along_axis(g_prob, g_sel[:, None], axis=-1)
    e_logits = (xt @ w_re + b_re).astype(jnp.float32).reshape(n_tok, N_GROUPS, EXPERTS_PER_GROUP)
    e_logits = jnp.take_along_axis(e_logits, g_sel[:, None, None], axis=1)[:, 0]
    top_v, top_i = lax.top_k(e_logits, TOP_K)
    e_w = jax.nn.softmax(top_v, axis=-1) * g_w
    expert_id = g_sel[:, None] * EXPERTS_PER_GROUP + top_i
    n_assign = n_tok * TOP_K
    flat_e = expert_id.reshape(-1)
    order = jnp.argsort(flat_e)
    sorted_e = flat_e[order]
    sorted_tok = order // TOP_K
    sorted_w = e_w.reshape(-1)[order]
    counts = jnp.bincount(flat_e, length=N_EXPERTS)
    starts = jnp.cumsum(counts) - counts
    padded = ((counts + EXPERT_BLOCK - 1) // EXPERT_BLOCK) * EXPERT_BLOCK
    pad_ends = jnp.cumsum(padded)
    pad_starts = pad_ends - padded
    dest = pad_starts[sorted_e] + jnp.arange(n_assign) - starts[sorted_e]
    n_blocks = -(-n_assign // EXPERT_BLOCK) + N_EXPERTS
    cap = n_blocks * EXPERT_BLOCK
    x_pad = jnp.zeros((cap, d), h.dtype).at[dest].set(xt[sorted_tok])
    block_e = jnp.minimum(
        jnp.searchsorted(pad_ends, jnp.arange(n_blocks) * EXPERT_BLOCK, side="right"), N_EXPERTS - 1)

    def run_block(args):
        xb, e = args
        return (jax.nn.silu(xb @ w_gate[e]) * (xb @ w_up[e])) @ w_down[e]

    y_pad = lax.map(run_block, (x_pad.reshape(n_blocks, EXPERT_BLOCK, d), block_e)).reshape(cap, d)
    y = y_pad[dest] * sorted_w[:, None].astype(h.dtype)
    out = jnp.zeros((n_tok, d), h.dtype).at[sorted_tok].add(y)
    return out.reshape(bsz, seq, d)

def first_inputs(seed: int = 0) -> dict:
    key = jax.random.key(seed)
    ks = jax.random.split(key, 28)
    L, D = DEPTH, D_MODEL
    nrm = lambda k, shape, s: jax.random.normal(k, shape, jnp.float32) * s
    return {
        "x": nrm(ks[0], (BATCH, SEQ, D), 1.0),
        "norm_mix_g": 1.0 + nrm(ks[1], (L, D), 0.02),
        "w_in": nrm(ks[2], (L, D, IN_COLS), D ** -0.5),
        "b_in": nrm(ks[3], (L, IN_COLS), 0.02),
        "conv_w": nrm(ks[4], (L, CONV_WIDTH, CONV_CH), CONV_WIDTH ** -0.5),
        "conv_b": nrm(ks[5], (L, CONV_CH), 0.02),
        "conv_ln_g": 1.0 + nrm(ks[6], (L, CONV_CH), 0.02),
        "conv_ln_b": nrm(ks[7], (L, CONV_CH), 0.02),
        "w_conv_out": nrm(ks[8], (L, CONV_CH, D), CONV_CH ** -0.5),
        "b_conv_out": nrm(ks[9], (L, D), 0.02),
        "sg_ln_g": 1.0 + nrm(ks[10], (L, SG_WIDTH), 0.02),
        "sg_ln_b": nrm(ks[11], (L, SG_WIDTH), 0.02),
        "w_sg": nrm(ks[12], (L, SG_HEADS, SG_BLOCK, SG_BLOCK), SG_BLOCK ** -0.5),
        "b_sg": 1.0 + nrm(ks[13], (L, SG_HEADS, SG_BLOCK), 0.02),
        "w_sg_out": nrm(ks[14], (L, SG_WIDTH, D), SG_WIDTH ** -0.5),
        "b_sg_out": nrm(ks[15], (L, D), 0.02),
        "w_out": nrm(ks[16], (L, D, D), D ** -0.5),
        "b_out": nrm(ks[17], (L, D), 0.02),
        "norm_ffn_g": 1.0 + nrm(ks[18], (L, D), 0.02),
        "w_router_group": nrm(ks[19], (L, D, N_GROUPS), D ** -0.5),
        "b_router_group": nrm(ks[20], (L, N_GROUPS), 0.01),
        "w_router_expert": nrm(ks[21], (L, D, N_EXPERTS), D ** -0.5),
        "b_router_expert": nrm(ks[22], (L, N_EXPERTS), 0.01),
        "w_expert_gate": nrm(ks[23], (L, N_EXPERTS, D, D_EXPERT), D ** -0.5),
        "w_expert_up": nrm(ks[24], (L, N_EXPERTS, D, D_EXPERT), D ** -0.5),
        "w_expert_down": nrm(ks[25], (L, N_EXPERTS, D_EXPERT, D), D_EXPERT ** -0.5),
        "norm_final_g": 1.0 + nrm(ks[26], (D,), 0.02),
    }

def first_block(x, norm_mix_g, w_in, b_in, conv_w, conv_b, conv_ln_g, conv_ln_b, w_conv_out, b_conv_out,
              sg_ln_g, sg_ln_b, w_sg, b_sg, w_sg_out, b_sg_out, w_out, b_out, norm_ffn_g,
              w_router_group, b_router_group, w_router_expert, b_router_expert,
              w_expert_gate, w_expert_up, w_expert_down, norm_final_g):
    for l in range(DEPTH):
        h = rms_norm(x, norm_mix_g[l])
        proj = h @ w_in[l] + b_in[l]
        a, z, gate_logits = jnp.split(proj, [2 * CONV_CH, 2 * CONV_CH + 2 * SG_WIDTH], axis=-1)
        y_a = conformer_conv_branch(a, conv_w[l], conv_b[l], conv_ln_g[l], conv_ln_b[l],
                                    w_conv_out[l], b_conv_out[l])
        y_b = spatial_gating_branch(z, sg_ln_g[l], sg_ln_b[l], w_sg[l], b_sg[l],
                                    w_sg_out[l], b_sg_out[l])
        g_a, g_b = jnp.split(jax.nn.sigmoid(gate_logits), 2, axis=-1)
        x = x + (g_a * y_a + g_b * y_b) @ w_out[l] + b_out[l]
        h = rms_norm(x, norm_ffn_g[l])
        x = x + hierarchical_moe(h, w_router_group[l], b_router_group[l], w_router_expert[l],
                                 b_router_expert[l], w_expert_gate[l], w_expert_up[l], w_expert_down[l])
    return rms_norm(x, norm_final_g)


DEPTH_2 = 2

N_META = 16
MIX_WIDTH = D_MODEL
ATTN_WIDTH = MIX_WIDTH // 2
CONV_WIDTH_2 = MIX_WIDTH - ATTN_WIDTH
HEAD_DIM = 64
N_Q_HEADS = ATTN_WIDTH // HEAD_DIM
N_KV_HEADS = 2
GROUP = N_Q_HEADS // N_KV_HEADS
KV_WIDTH = N_KV_HEADS * HEAD_DIM
CONV_GROUPS = 8
CONV_K = 3
WINDOW = 128
BLOCK = 128
LEAD_PAD = BLOCK - N_META
ROPE_THETA = 500000.0
ROT_DIM = HEAD_DIM // 4
D_FF = 4 * D_MODEL
IN_WIDTH = ATTN_WIDTH + 2 * KV_WIDTH + 3 * CONV_WIDTH_2


def rmsnorm(x, g):
    x32 = x.astype(jnp.float32)
    y = x32 * lax.rsqrt(jnp.mean(x32 * x32, axis=-1, keepdims=True) + EPS)
    return y.astype(x.dtype) * g.astype(x.dtype)

def rope_tables(n_pos):
    pos = jnp.arange(n_pos, dtype=jnp.float32)
    inv_freq = jnp.power(jnp.float32(ROPE_THETA), -jnp.arange(0, ROT_DIM, 2, dtype=jnp.float32) / ROT_DIM)
    ang = pos[:, None] * inv_freq[None, :]
    return jnp.cos(ang), jnp.sin(ang)

def partial_rope(t, cos, sin):
    half = ROT_DIM // 2
    t32 = t[..., :ROT_DIM].astype(jnp.float32)
    t1, t2 = t32[..., :half], t32[..., half:]
    c, s = cos[None, :, None, :], sin[None, :, None, :]
    rot = jnp.concatenate([t1 * c - t2 * s, t2 * c + t1 * s], axis=-1).astype(t.dtype)
    return jnp.concatenate([rot, t[..., ROT_DIM:]], axis=-1)

def sliding_window_gqa_sinks(q, k, v, sink):
    bsz, L = q.shape[0], q.shape[1]
    pad = ((0, 0), (LEAD_PAD, 0), (0, 0), (0, 0))
    q, k, v = jnp.pad(q, pad), jnp.pad(k, pad), jnp.pad(v, pad)
    Lp = L + LEAD_PAD
    nb = Lp // BLOCK
    qb = q.reshape(bsz, nb, BLOCK, N_KV_HEADS, GROUP, HEAD_DIM)

    def band(t):
        tb = t.reshape(bsz, nb, BLOCK, N_KV_HEADS, HEAD_DIM)
        prev = jnp.pad(tb, ((0, 0), (1, 0), (0, 0), (0, 0), (0, 0)))[:, :-1]
        return jnp.concatenate([prev, tb], axis=2)

    kw, vw = band(k), band(v)
    s = jnp.einsum('bnqhgd,bnkhd->bnhgqk', qb, kw,
                   preferred_element_type=jnp.float32) * (HEAD_DIM ** -0.5)
    blk = jnp.arange(nb)[:, None, None]
    qpos = blk * BLOCK + jnp.arange(BLOCK)[None, :, None]
    kpos = (blk - 1) * BLOCK + jnp.arange(2 * BLOCK)[None, None, :]
    mask = (kpos <= qpos) & (qpos - kpos < WINDOW) & (kpos >= LEAD_PAD)
    s = jnp.where(mask[None, :, None, None], s, -jnp.inf)
    sk = sink.astype(jnp.float32).reshape(1, 1, N_KV_HEADS, GROUP, 1, 1)
    m = jnp.maximum(jnp.max(s, axis=-1, keepdims=True), sk)
    e = jnp.exp(s - m)
    p = e / (jnp.sum(e, axis=-1, keepdims=True) + jnp.exp(sk - m))
    o = jnp.einsum('bnhgqk,bnkhd->bnqhgd', p.astype(v.dtype), vw)
    return o.reshape(bsz, Lp, N_Q_HEADS * HEAD_DIM)[:, LEAD_PAD:]

def short_gated_conv(b_gate, c_gate, h, w):
    u = c_gate * h
    y = lax.conv_general_dilated(u, w[:, None, :].astype(u.dtype), window_strides=(1,),
                                 padding=[(CONV_K - 1, 0)],
                                 dimension_numbers=('NWC', 'WIO', 'NWC'),
                                 feature_group_count=CONV_WIDTH_2)
    return b_gate * y

def second_inputs(seed: int = 0) -> dict:
    key = jax.random.key(seed)
    ks = jax.random.split(key, 16)
    f32 = jnp.float32

    def nrm(k, shape, scale):
        return jax.random.normal(k, shape, f32) * scale

    def gain(k, shape):
        return 1.0 + 0.05 * jax.random.normal(k, shape, f32)

    return {
        'x': nrm(ks[0], (BATCH, SEQ, D_MODEL), 1.0),
        'meta_tokens': nrm(ks[1], (N_META, D_MODEL), 1.0),
        'mix_pre_g': gain(ks[2], (DEPTH_2, D_MODEL)),
        'w_in': nrm(ks[3], (DEPTH_2, D_MODEL, IN_WIDTH), D_MODEL ** -0.5),
        'conv_w': nrm(ks[4], (DEPTH_2, CONV_K, CONV_WIDTH_2), CONV_K ** -0.5),
        'sinks': nrm(ks[5], (DEPTH_2, N_Q_HEADS), 0.5),
        'attn_out_g': gain(ks[6], (DEPTH_2, ATTN_WIDTH)),
        'conv_out_g': gain(ks[7], (DEPTH_2, CONV_WIDTH_2)),
        'w_out': nrm(ks[8], (DEPTH_2, MIX_WIDTH, D_MODEL), MIX_WIDTH ** -0.5),
        'mix_post_g': gain(ks[9], (DEPTH_2, D_MODEL)),
        'mlp_pre_g': gain(ks[10], (DEPTH_2, D_MODEL)),
        'w_up': nrm(ks[11], (DEPTH_2, D_MODEL, D_FF), D_MODEL ** -0.5),
        'w_down': nrm(ks[12], (DEPTH_2, D_FF, D_MODEL), D_FF ** -0.5),
        'mlp_post_g': gain(ks[13], (DEPTH_2, D_MODEL)),
    }

def second_block(x, meta_tokens, mix_pre_g, w_in, conv_w, sinks, attn_out_g, conv_out_g,
              w_out, mix_post_g, mlp_pre_g, w_up, w_down, mlp_post_g):
    bsz = x.shape[0]
    meta = jnp.broadcast_to(meta_tokens[None].astype(x.dtype), (bsz, N_META, D_MODEL))
    h = jnp.concatenate([meta, x], axis=1)
    L = h.shape[1]
    cos, sin = rope_tables(L)
    s_q = ATTN_WIDTH
    s_k = s_q + KV_WIDTH
    s_v = s_k + KV_WIDTH
    s_b = s_v + CONV_WIDTH_2
    s_c = s_b + CONV_WIDTH_2
    for l in range(DEPTH_2):
        a = rmsnorm(h, mix_pre_g[l])
        proj = a @ w_in[l]
        q = proj[..., :s_q].reshape(bsz, L, N_Q_HEADS, HEAD_DIM)
        k = proj[..., s_q:s_k].reshape(bsz, L, N_KV_HEADS, HEAD_DIM)
        v = proj[..., s_k:s_v].reshape(bsz, L, N_KV_HEADS, HEAD_DIM)
        b_gate = proj[..., s_v:s_b]
        c_gate = proj[..., s_b:s_c]
        hc = proj[..., s_c:]
        q = partial_rope(q, cos, sin)
        k = partial_rope(k, cos, sin)
        y_attn = sliding_window_gqa_sinks(q, k, v, sinks[l])
        y_conv = short_gated_conv(b_gate, c_gate, hc, conv_w[l])
        y = jnp.concatenate([rmsnorm(y_attn, attn_out_g[l]),
                             rmsnorm(y_conv, conv_out_g[l])], axis=-1)
        h = h + rmsnorm(y @ w_out[l], mix_post_g[l])
        a = rmsnorm(h, mlp_pre_g[l])
        f = jnp.square(jax.nn.relu(a @ w_up[l])) @ w_down[l]
        h = h + rmsnorm(f, mlp_post_g[l])
    return h[:, N_META:]


def setup_inputs(seed=0):
    out = dict(first_inputs(seed))
    for name, value in second_inputs(seed + 1).items():
        if name != "x":
            out[name + "_2"] = value
    return out


def reference(
    x, norm_mix_g, w_in, b_in, conv_w, conv_b, conv_ln_g, conv_ln_b, w_conv_out, b_conv_out,
    sg_ln_g, sg_ln_b, w_sg, b_sg, w_sg_out, b_sg_out, w_out, b_out, norm_ffn_g, w_router_group,
    b_router_group, w_router_expert, b_router_expert, w_expert_gate, w_expert_up, w_expert_down,
    norm_final_g, meta_tokens_2, mix_pre_g_2, w_in_2, conv_w_2, sinks_2, attn_out_g_2,
    conv_out_g_2, w_out_2, mix_post_g_2, mlp_pre_g_2, w_up_2, w_down_2, mlp_post_g_2,
):
    x = first_block(
        x, norm_mix_g, w_in, b_in, conv_w, conv_b, conv_ln_g, conv_ln_b, w_conv_out, b_conv_out,
        sg_ln_g, sg_ln_b, w_sg, b_sg, w_sg_out, b_sg_out, w_out, b_out, norm_ffn_g,
        w_router_group, b_router_group, w_router_expert, b_router_expert, w_expert_gate,
        w_expert_up, w_expert_down, norm_final_g,
    )
    return second_block(
        x, meta_tokens_2, mix_pre_g_2, w_in_2, conv_w_2, sinks_2, attn_out_g_2, conv_out_g_2,
        w_out_2, mix_post_g_2, mlp_pre_g_2, w_up_2, w_down_2, mlp_post_g_2,
    )


_drawn_inputs = setup_inputs


def setup_inputs(seed=0):
    import zlib

    import numpy as np

    out = dict(_drawn_inputs(seed))
    spreads = {}
    factors = {'sg_ln_g': 8.712,
     'b_sg': 18.482,
     'b_router_group': 50.854,
     'b_router_expert': 31.675,
     'sinks_2': 8.0,
     'conv_b': 3.312,
     'conv_ln_g': 5.864,
     'conv_ln_b': 6.898,
     'b_conv_out': 2.813,
     'sg_ln_b': 23.046,
     'b_sg_out': 3.339,
     'b_out': 3.79,
     'norm_ffn_g': 5.009}
    for name, (base, spread) in spreads.items():
        noise = np.random.default_rng([zlib.crc32(name.encode()), seed]).standard_normal(out[name].shape)
        drawn = base * np.exp(spread * noise) if base else spread * noise
        out[name] = __import__('jax').numpy.asarray(drawn.astype(out[name].dtype))
    for name, factor in factors.items():
        out[name] = (out[name] * factor).astype(out[name].dtype)
    return out
```

```python
from contextlib import ExitStack

import numpy as np

import concourse.bass as bass
from concourse import mybir

ALU = mybir.AluOpType
ACT = mybir.ActivationFunctionType
F32 = mybir.dt.float32
F32R = mybir.dt.float32r
I32 = mybir.dt.int32
AX_X = mybir.AxisListType.X

P = 128
D = 1024
KC = D // P
T = 512
NT = T // P
TAPS = 31
PAD = TAPS - 1
HEADS_SG = 8
GROUPS, PER_GROUP = 4, 8
EXPERTS = GROUPS * PER_GROUP
ROUTER = GROUPS + EXPERTS
EXTRA = 2 * T // P - 1
BLOCKS = EXPERTS + EXTRA
UNUSED = 4096
EPS = 1e-6

LAYERS = 2
META = 16
L = T + META
HALF = L // 2
AC = 4
QB = 5
HD = 64
QUARTERS = 4
MASKED = -1.0e30

UNIT = 1024
RAW = 8
SPLIT = 4
AHEAD = SPLIT - 1
U_A2, U_A1, U_V, U_U, U_GA, U_GB, U_SGO, U_CVO, U_OUT = range(0, 72, 8)
U_MOE = 72
PER_EXPERT = 12
U_LAST = U_MOE + EXPERTS * PER_EXPERT
U_LAYER = U_LAST + 8
PER_LAYER = 96
U_END = U_LAYER + LAYERS * PER_LAYER
UNITS = U_END + 8
DVE_CONV = 6
TAPS_PER_STEP = 5
CHAIN = 103
L_OUT, L_MLP, L_DUMMY = 18, 26, 90

COLS = {}
_n = 0
for _name, _w in (("norm_mix_g", 8), ("b_in", 48), ("conv_w", 8 * TAPS), ("conv_b", 8), ("conv_ln_g", 8),
                  ("conv_ln_b", 8), ("b_conv_out", 8), ("sg_ln_g", 8), ("sg_ln_b", 8), ("b_sg_out", 8),
                  ("b_out", 8), ("norm_ffn_g", 8), ("norm_final_g", 8)):
    COLS[_name] = _n
    _n += _w
NPAR = _n
LCOLS = {}
_n = 0
for _name, _w in (("mix_pre", 8), ("attn_g", 4), ("conv_g", 4), ("mix_post", 8), ("mlp_pre", 8),
                  ("mlp_post", 8), ("conv_w", 12), ("sinks", 8)):
    LCOLS[_name] = _n
    _n += _w
NLPAR = _n

C_IDENT, C_BEFORE, C_ONE, C_MEAN, C_IOTA = 0, 128, 256, 384, 512
C_TOK = 640
C_GTOK = 648
C_STOK = 656
C_EPS = 664
NCONST = 665
D_MEAN, D_MEAN2, D_IDENT, D_ROT, D_COS, D_SIN = 0, 128, 256, 384, 512, 512 + L
D_MASK = (D_SIN + L, D_SIN + L + 16, D_SIN + L + 16 + 144)
D_EPS = D_MASK[2] + 256
NCONST2 = D_EPS + 1


FROM = {"silu_done": 1, "yb_ready": 1, "u_free": 1, "rot_used": 1, "kv_ready": 1,
        "pt_free": 1, "mk_ready": 1, "at2_ready": 1, "om_ready": 1, "pv_done": 1, "fr_done": 1}


class Count:

    def __init__(self, eng, sem):
        self.eng, self.sem, self.base, self.n = eng, sem, 0, 0

    def add(self, ins):
        ins.then_inc(self.sem, 1)
        self.n += 1

    def wait(self, back=0):
        need(self.eng, self.sem, self.base + self.n - back)

    def loop(self, index, first, per):
        self.start, self.per = self.n, per
        self.base, self.first = self.base + (index - first) * per, first

    def end(self, times):
        assert self.n - self.start == self.per, (self.n - self.start, self.per)
        self.base, self.n = 0, self.start + times * self.per


def need(eng, sem, value):
    if not isinstance(value, int) or value > 0:
        eng.wait_ge(sem, value)


def program(nc, W, xT, par, lpar, cst, cst2, bv, bs, wsT, wr, rb, metaT, out):
    with ExitStack() as ctx:
        def sem(name):
            return ctx.enter_context(nc.semaphore(name))


        start = nc.sbuf_base + (-nc.sbuf_base) % 64
        size = (nc.sbuf_usable_end - start) // 64 * 64
        ctx.enter_context(nc.sbuf_tensor("arena", [P, size // 4], F32, align_bytes=64))
        where = {}

        class Map:

            def __init__(self, at):
                self.at = at

            def put(self, name, shape, dt=F32):
                n = 4
                for s in shape[1:]:
                    n *= s
                where[name] = self.at
                t = nc.alloc_sbuf_tensor_at(name, shape, dt, offset=self.at)
                self.at += (n + 63) // 64 * 64
                assert self.at <= start + size, (name, self.at - start - size)
                return t

        m = Map(start)
        raw = m.put("raw", [P, RAW, UNIT])
        w_hi = m.put("w_hi", [P, SPLIT, UNIT], F32R)
        w_lo = m.put("w_lo", [P, SPLIT, UNIT], F32R)
        x_hi = m.put("x_hi", [P, KC, L], F32R)
        x_lo = m.put("x_lo", [P, KC, L], F32R)
        low = m.at

        m = Map(low)
        pars = m.put("pars", [P, NPAR])
        consts = m.put("consts", [P, NCONST])
        y1 = m.put("y1", [P, KC, T])
        top = m.at
        stage = m.put("stage", [P, KC, T])
        apad = m.put("apad", [P, KC, T + PAD])
        ubuf = m.put("ubuf", [P, KC, T])
        gate_a = m.put("gate_a", [P, KC, T])
        bs_sb = m.put("bs_sb", [P, HEADS_SG, P])
        ws_sb = m.put("ws_sb", [P, HEADS_SG, P])
        val = m.put("val", [P, 3, T])
        sq = m.put("sq", [P, 2, T])
        rstd = m.put("rstd", [P, T])
        mu = m.put("mu", [P, T])
        vst = m.put("vst", [P, NT, 2, 6])
        vmv = m.put("vmv", [P, NT, 2])
        vrs = m.put("vrs", [P, NT])
        bv_sb = Map(where["gate_a"]).put("bv_sb", [P, D])
        xr = Map(where["apad"]).put("xr", [P, KC, T])
        vtok = stage[:, :, :].rearrange("p c t -> p (c t)").rearrange("p (n d) -> p n d", n=NT)

        m = Map(top)
        hb = m.put("hb", [P, KC, T])
        htok = m.put("htok", [P, NT, D])
        rsq = m.put("rsq", [P, 2, T])
        rrs = m.put("rrs", [P, T])
        wr_sb = m.put("wr_sb", [P, KC, ROUTER])
        rb_sb = m.put("rb_sb", [P, ROUTER])
        lg = m.put("lg", [P, NT, ROUTER])
        rt = m.put("rt", [P, 12, NT, EXPERTS])
        rs = m.put("rs", [P, 32, NT])
        onr = m.put("onr", [P, 2, P])
        onb = m.put("onb", [P, 2, 2 * BLOCKS])
        idx = m.put("idx", [P, 2 * BLOCKS], I32)
        eint = m.put("eint", [P, EXTRA + 1], I32)
        wts = m.put("wts", [P, 2, NT])
        xt_hi = m.put("xt_hi", [P, 2, KC, P], F32R)
        xt_lo = m.put("xt_lo", [P, 2, KC, P], F32R)
        gs = m.put("gs", [P, T])
        ab = m.put("ab", [P, T])
        at_hi = m.put("at_hi", [P, 2, 4, P], F32R)
        at_lo = m.put("at_lo", [P, 2, 4, P], F32R)
        yb = m.put("yb", [P, 2, D])
        y2b = Map(where["hb"]).put("y2b", [P, 2, 2, D])
        m = Map(where["htok"])
        xg = m.put("xg", [P, 2, D])
        ot2 = m.put("ot2", [P, 2, D])
        bg = Map(where["x_hi"]).put("bg", [P, 4, UNIT])
        bu = Map(where["x_lo"]).put("bu", [P, 4, UNIT])
        bd = Map(where["hb"]).put("bd", [P, 4, UNIT])
        bx = Map(where["ot2"]).put("bx", [P, KC, P])
        ba = Map(where["at_hi"]).put("ba", [P, 4, P])

        m = Map(low)
        lp = m.put("lp", [P, NLPAR])
        k_hi = m.put("k_hi", [P, KC, L], F32R)
        k_lo = m.put("k_lo", [P, KC, L], F32R)
        res = m.put("res", [P, KC, L])
        fb = m.put("fb", [P, KC, L])
        c2 = m.put("c2", [P, NCONST2])
        kb = m.put("kb", [P, L])
        vb = m.put("vb", [P, QB, P])
        sc = m.put("sc", [P, 2, 4, 256])
        pt = m.put("pt", [P, 2, 2, 4, P])
        ot = m.put("ot", [P, 2, 8, HD])
        val2 = m.put("val2", [P, 3, L])
        sq2 = m.put("sq2", [P, 2, L])
        rstd2 = Map(where["kb"]).put("rstd2", [P, L])
        sm = m.put("sm", [P, 4, 6, 4])
        orr = m.put("orr", [P, 4])
        m = Map(where["fb"])
        qb = m.put("qb", [P, AC, L])
        bb = m.put("bb", [P, AC, L])
        m = Map(where["k_hi"])
        cb = m.put("cb", [P, AC, L])
        up = m.put("up", [P, AC, L + 2])
        yat = m.put("yat", [P, AC, L])
        rot = m.put("rot", [P, L])
        rl = Map(where["sc"]).put("rl", [P, 2, L])
        assert where["res"] >= where["y1"] + 4 * KC * T

        dense = [ctx.enter_context(nc.psum_tensor(f"dense{i}", [P, 2, 512], F32)) for i in range(2)]
        pair = ctx.enter_context(nc.psum_tensor("pair", [P, 2, 512], F32))
        duo = ctx.enter_context(nc.psum_tensor("duo", [P, 2, 512], F32))
        hrows = nc.dram_tensor("hrows", [T, D], F32).ap()
        y2 = nc.dram_tensor("y2", [2 * T, D], F32).ap()

        names = """raw_in0 raw_in1 raw_in2 raw_in3 x_in const_in aux_in mask_in xr_in meta_in lpar_in out_done
            hi_done w_ready unit_done dense_free0 dense_free1 phase sq_ready sq_used val_ready xh_done
            x_ready dve_chain pool_chain v_sum v_gelu vn_ready rows_done sp_done sp_free
            conv_done s1_done pconv_done fb_zero yc_ready t_ready hb_ready lg_done tr_done ht_ready hrows_in ge_ready
            rank_ready rank_done list_ready list_done idx_ready xg_in0 xg_in1 xt_done xth_done xt_ready
            silu_done u_free ath_done at_ready yb_ready ys_out0 ys_out1 bx_in bw_in bx_done bx_ready
            bgu_done bs_done ba_ready bat_done bat_ready bd_done by_ready by_out y2_in0 y2_in1 o2_ready
            o2_done x2_ready res_ready rot_done rot_used kv_ready mk_ready ex_done sc_done pt_done
            pt_free pv_done o_ready at2_ready cv_ready fr_done root_ready ms_ready om_ready os_ready bg_ready gx_ready pad_ready""".split()
        S = {n: sem(n) for n in names}
        raw_in = [S[f"raw_in{i}"] for i in range(4)]
        dense_free = [S["dense_free0"], S["dense_free1"]]
        xg_in = [S["xg_in0"], S["xg_in1"]]
        ys_out = [S["ys_out0"], S["ys_out1"]]
        y2_in = [S["y2_in0"], S["y2_in1"]]
        block = ctx.enter_context(nc.Block())

        def col(name, i):
            return pars[:, COLS[name] + i:COLS[name] + i + 1]

        def lcol(name, i, n=1):
            return lp[:, LCOLS[name] + i:LCOLS[name] + i + n]

        halves = ((0, HALF), (HALF, HALF))
        whole = ((0, T),)
        FEED = 56
        USES = 45
        SQS = 36
        VALS = 52
        STEPS = 14

        def item(i):
            n, g = i // 2, i % 2
            q0 = 0 if n == 0 else META + P * (n - 1)
            own = (n, q0, META if n == 0 else P)
            keys = [own] if n == 0 else [(n - 1, max(q0 - P, 0), META if n == 1 else P), own]
            return n, g, q0, own[2], keys

        pt_order = []
        for s in range(STEPS):
            if s >= 5 and s % 2 == 1:
                pt_order.append((s - 5) // 2)
            if 0 <= s - 1 < 10:
                pt_order += [(s - 1, 0), (s - 1, 1)]
        PTS = len(pt_order)
        ptseq = lambda i, hp: pt_order.index((i, hp))
        atseq = lambda n: pt_order.index(n)

        class Part:

            def __init__(self, u, u8=None):
                self.u, self.u8 = u, u // RAW if u8 is None else u8

        MOE = lambda k: Part(U_MOE + k * 24, U_MOE // RAW + k * 3)
        LAYER = lambda l, q=0: Part(U_LAYER + l * PER_LAYER + q * 16, U_LAYER // RAW + l * (PER_LAYER // RAW) + q * 2)


        @block.sync
        def _(sp):
            sp.dma_start(stage[:, :, :], xT).then_inc(S["x_in"], 16)
            sp.dma_start(pars[:, :], par).then_inc(S["const_in"], 16)
            sp.dma_start(consts[:, :], cst).then_inc(S["const_in"], 16)
            for i in range(4):
                sp.dma_start(raw[:, 2 * i:2 * i + 2, :],
                             W[2 * i:2 * i + 2].rearrange("u p n -> p u n")).then_inc(raw_in[i], 16)
            with sp.Fori(1, UNITS // RAW) as r:
                for i in range(4):
                    sp.wait_ge(S["w_ready"], (r - 1) * RAW + 2 * i + 2)
                    sp.dma_start(raw[:, 2 * i:2 * i + 2, :],
                                 W[bass.ds(r * RAW + 2 * i, 2)].rearrange("u p n -> p u n")).then_inc(raw_in[i], 16)
            sp.wait_ge(S["fr_done"], 8 * LAYERS + 1)
            sp.dma_start(out, res[:, :, META:]).then_inc(S["out_done"], 16)
            sp.wait_ge(S["out_done"], 16)

        def barrier(eng, n):
            eng.drain().then_inc(S["phase"], 1)
            eng.wait_ge(S["phase"], 4 * n)

        @block.gpsimd
        def _(pool):
            pc = Count(pool, S["pool_chain"])
            pool.dma_start(bv_sb[:, :], bv).then_inc(S["aux_in"], 16)
            pool.dma_start(bs_sb[:, :, :], bs).then_inc(S["aux_in"], 16)
            pool.dma_start(ws_sb[:, :, :], wsT).then_inc(S["aux_in"], 16)
            pc.add(pool.memset(apad[:, :, 0:PAD], 0.0))
            pool.wait_ge(S["aux_in"], 48)
            pc.wait()
            pc.add(pool.memset(ws_sb[64:128, :, 0:64], 0.0))
            pc.wait()
            pool.wait_ge(S["sq_used"], KC)
            own = range(DVE_CONV, KC)
            for k in range(TAPS):
                for c in own:
                    wc = col("conv_w", c * TAPS + k)
                    src = apad[:, c, k:k + T]
                    if k == 0:
                        pool.wait_ge(dense_free[c % 2], (U_A1 + c) // 2 + 1)
                        pc.add(pool.tensor_scalar(y1[:, c, :], src, wc, col("conv_b", c), ALU.mult, ALU.add))
                    else:
                        pc.add(pool.tensor_scalar(sq[:, c % 2, :], src, wc, None, ALU.mult))
                if k:
                    for c in own:
                        pc.wait(len(own) - 1)
                        pc.add(pool.tensor_tensor(y1[:, c, :], y1[:, c, :], sq[:, c % 2, :], ALU.add))
                pc.wait()
            pool.drain().then_inc(S["pconv_done"], 1)
            pool.wait_ge(S["conv_done"], DVE_CONV * TAPS)
            pool.dma_start(xr[:, :, :], xT).then_inc(S["xr_in"], 16)
            pool.wait_ge(S["xr_in"], 16)
            barrier(pool, 1)

            pool.dma_start(wr_sb[:, :, :], wr).then_inc(S["mask_in"], 16)
            pool.dma_start(rb_sb[:, :], rb).then_inc(S["mask_in"], 16)
            pool.wait_ge(S["hrows_in"], 16 * NT)
            pc.add(pool.memset(xg[:, :, :], 0.0))
            pc.wait()

            def gather(e):
                if e >= 2:
                    pool.wait_ge(S["xt_done"], e - 1)
                if e == 0:
                    pool.wait_ge(S["idx_ready"], 1)
                pool.indirect_dma_start(
                    out=xg[:, e % 2, :], out_offset=None, in_=hrows,
                    in_offset=bass.IndirectOffsetOnAxis(ap=idx[:, e:e + 1], axis=0),
                    bounds_check=T - 1, oob_is_err=False).then_inc(xg_in[e % 2], 16)

            def scatter(e, src, done):
                pool.indirect_dma_start(
                    out=y2, out_offset=bass.IndirectOffsetOnAxis(ap=idx[:, BLOCKS + e:BLOCKS + e + 1], axis=0),
                    in_=src, in_offset=None,
                    bounds_check=2 * T - 1, oob_is_err=False).then_inc(done, 16)

            gather(0)
            gather(1)
            gather(2)
            for s in range(1, EXPERTS + 1):
                if s + 2 <= EXPERTS:
                    gather(s + 2)
                pool.wait_ge(S["yb_ready"], s + 2)
                scatter(s - 1, yb[:, s % 2, :], ys_out[s % 2])
            pool.wait_ge(ys_out[1], 16 * EXPERTS // 2)
            pool.wait_ge(ys_out[0], 16 * EXPERTS // 2)
            pool.wait_ge(S["xt_done"], EXPERTS + 1)
            extra = pool.value_load(eint[0:1, EXTRA:EXTRA + 1])
            for b in range(EXTRA):
                with pool.If(extra > b):
                    pool.indirect_dma_start(
                        out=xg[:, 0, :], out_offset=None, in_=hrows,
                        in_offset=bass.IndirectOffsetOnAxis(ap=idx[:, EXPERTS + b:EXPERTS + b + 1], axis=0),
                        bounds_check=T - 1, oob_is_err=False).then_inc(S["bx_in"], 16)
                    pool.wait_ge(S["by_ready"], b + 1)
                    scatter(EXPERTS + b, yb[:, 0, :], S["by_out"])
                    pool.wait_ge(S["by_out"], 16 * (b + 1))
            for t in range(NT):
                if t >= 2:
                    pool.wait_ge(S["o2_ready"], t - 1)
                pool.dma_start(y2b[:, t % 2, :, :],
                               y2[2 * t * P:2 * (t + 1) * P, :].rearrange("(p j) d -> p j d", j=2)
                               ).then_inc(y2_in[t % 2], 16)
            barrier(pool, 2)
            pool.dma_start(res[:, :, 0:META], metaT).then_inc(S["meta_in"], 16)
            pool.dma_start(c2[:, :], cst2).then_inc(S["meta_in"], 16)
            pool.wait_ge(S["meta_in"], 32)
            barrier(pool, 3)
            with pool.Fori(0, LAYERS) as l:
                need(pool, S["fr_done"], l * 8 + 1)
                pool.dma_start(lp[:, :], lpar[l]).then_inc(S["lpar_in"], 16)
                pool.memset(up[:, :, 0:2], 0.0).then_inc(S["pad_ready"], 1)
                mixed = pool.to_reg(l * 8 + 8)
                pool.wait_ge(S["meta_in"], 32)
                pool.wait_ge(S["res_ready"], mixed)
                pool.memset(fb[:, :, :], 0.0).then_inc(S["fb_zero"], 1)
        @block.tensor
        def _(pe):
            def dense_unit(w, j, use, which, parts, hi, lo, fed=None):
                need(pe, S["w_ready"], w.u + j + 1)
                need(pe, dense_free[which], use)
                s = j % SPLIT
                for kc in range(KC):
                    if fed is not None:
                        need(pe, S["x_ready"], fed + kc + 1)
                    c = slice(kc * P, (kc + 1) * P)
                    for wt, x in ((w_hi, hi), (w_hi, lo), (w_lo, hi)):
                        for h, (t0, n) in enumerate(parts):
                            last = pe.matmul(dense[which][:, h, 0:n], wt[:, s, c], x[:, kc, t0:t0 + n],
                                             start=(kc == 0 and wt is w_hi and x is hi),
                                             stop=(kc == KC - 1 and wt is w_lo))
                last.then_inc(S["unit_done"], 1)

            def sums(chunks, n0, ones, src, parts, ready="sq_ready", used="sq_used", only=None):
                for c in range(chunks) if only is None else only:
                    need(pe, S[ready], n0 + c + 1)
                    for h, (t0, n) in enumerate(parts):
                        last = pe.matmul(pair[:, h, 0:n], ones, src(c)[:, t0:t0 + n], start=(c == 0), stop=(c == chunks - 1))
                    last.then_inc(S[used], 1)

            pe.drain().then_inc(S["pv_done"], FROM["pv_done"])
            mean = consts[:, C_MEAN:C_MEAN + P]
            ident = consts[:, C_IDENT:C_IDENT + P]
            pe.wait_ge(S["const_in"], 32)
            sums(KC, 0, mean, lambda c: sq[:, c % 2, :], whole)

            def run(u0, fed=None):
                for m in range(8):
                    d = (u0 if u0 < U_V else u0 - 8) + m
                    dense_unit(Part(u0), m, d // 2, d % 2, whole, x_hi, x_lo, fed if m == 0 else None)

            run(U_A2, fed=0)
            run(U_A1)
            for h in range(2):
                for i in range(2):
                    need(pe, dense_free[i], 8)
                for j in range(4):
                    u = U_V + 4 * h + j
                    need(pe, S["w_ready"], u + 1)
                    for kk in range(2):
                        kc = 2 * j + kk
                        for t in range(NT):
                            bank = (dense[0], dense[1], pair, duo)[2 * h + t // 2][:, t % 2, :]
                            for x, wt in ((x_hi, w_hi), (x_hi, w_lo), (x_lo, w_hi)):
                                last = pe.matmul(bank, x[:, kc, t * P:(t + 1) * P], wt[:, u % SPLIT, kk * 512:(kk + 1) * 512],
                                                 start=(kc == 0 and x is x_hi and wt is w_hi), stop=(kc == KC - 1 and x is x_lo))
                    last.then_inc(S["unit_done"], 1)
            pe.wait_ge(S["v_sum"], 4)
            run(U_U)
            pe.wait_ge(S["v_sum"], 8)
            pe.wait_ge(S["pool_chain"], 2)
            for h in range(2):
                last = pe.matmul(pair[:, h, :], consts[:, C_ONE:C_ONE + P],
                                 ws_sb[:, 4 * h:4 * h + 4, :].rearrange("p h q -> p (h q)"), start=True, stop=True)
            last.then_inc(S["rows_done"], 1)
            pe.wait_ge(S["vn_ready"], NT)
            for m in range(8):
                d = U_GA - 8 + m
                dense_unit(Part(U_GA), m, d // 2, d % 2, whole, x_hi, x_lo)
                need(pe, S["sp_free"], m - 1)
                for n in range(NT):
                    last = pe.matmul(duo[:, m % 2, n * P:(n + 1) * P], vtok[:, n, m * P:(m + 1) * P], ws_sb[:, m, :],
                                     start=True, stop=True)
                last.then_inc(S["sp_done"], 1)
            run(U_GB - 0)
            pe.wait_ge(S["sp_free"], 8)
            for m in range(8):
                d = U_SGO - 8 + m
                dense_unit(Part(U_SGO), m, d // 2, d % 2, whole, x_hi, x_lo, 8 if m == 0 else None)
                if m == 1:
                    pe.wait_ge(S["conv_done"], DVE_CONV * TAPS)
                    pe.wait_ge(S["pconv_done"], 1)
                    sums(KC, -KC, mean, lambda c: y1[:, c, :], whole, used="s1_done")
                if m == 4:
                    sums(KC, KC, mean, lambda c: sq[:, c % 2, :], whole)
            run(U_CVO, fed=16)
            run(U_OUT, fed=24)
            barrier(pe, 1)

            sums(KC, 2 * KC, mean, lambda c: rsq[:, c % 2, :], whole)
            pe.wait_ge(S["hb_ready"], KC)
            pe.wait_ge(S["mask_in"], 32)
            for t in range(NT):
                for kc in range(KC):
                    last = pe.matmul(duo[:, 0, t * ROUTER:(t + 1) * ROUTER], hb[:, kc, t * P:(t + 1) * P], wr_sb[:, kc, :],
                                     start=(kc == 0), stop=(kc == KC - 1))
            last.then_inc(S["lg_done"], 1)
            for t in range(NT):
                need(pe, S["ht_ready"], t - 1)
                for c in range(KC):
                    last = pe.transpose(dense[t % 2][:, c // 4, (c % 4) * P:(c % 4 + 1) * P], hb[:, c, t * P:(t + 1) * P], ident)
                last.then_inc(S["tr_done"], 1)
            pe.wait_ge(S["rank_ready"], 1)
            msum = rt[:, 6, :, :]
            for t in range(NT + 1):
                for s in range(min(t + 1, NT)):
                    lhs = C_BEFORE if s == t else C_ONE
                    last = pe.matmul(duo[:, 1, t * EXPERTS:(t + 1) * EXPERTS], consts[:, lhs:lhs + P], msum[:, s, :],
                                     start=(s == 0), stop=(s == min(t, NT - 1)))
            last.then_inc(S["rank_done"], 1)
            for k in range(2 * NT):
                pe.wait_ge(S["list_ready"], k + 1)
                pe.matmul(duo[:, 0, 0:2 * BLOCKS], onr[:, k % 2, :], onb[:, k % 2, :],
                          start=(k == 0), stop=(k == 2 * NT - 1)).then_inc(S["list_done"], 1)

            def rows_to_columns(e, par):
                need(pe, xg_in[par], 16 * (e // 2 + 1) if isinstance(e, int) else 16 * e)
                for c in range(KC):
                    last = pe.transpose(pair[:, c // 4, (c % 4) * P:(c % 4 + 1) * P], xg[:, par, c * P:(c + 1) * P], ident)
                last.then_inc(S["xt_done"], 1)

            rows_to_columns(0, 0)

            def expert(k, w, par):
                e = 2 * k + par
                j0 = PER_EXPERT * par
                pe.wait_ge(S["xt_ready"], e + 1)
                for j in range(8):
                    if j == 0:
                        need(pe, S["silu_done"], e + 1)
                    if j == 4:
                        need(pe, xg_in[1 - par], 16 * (k + 1 + par))
                        for c in range(KC):
                            last = pe.transpose(pair[:, c // 4, (c % 4) * P:(c % 4 + 1) * P],
                                                xg[:, 1 - par, c * P:(c + 1) * P], ident)
                        last.then_inc(S["xt_done"], 1)
                        need(pe, S["u_free"], e + 1)
                    s = (j0 + j) % SPLIT
                    pe.wait_ge(S["w_ready"], w.u + j0 + j + 1)
                    for kk in range(2):
                        kc = (2 * j + kk) % KC
                        for x, wt in ((xt_hi, w_hi), (xt_hi, w_lo), (xt_lo, w_hi)):
                            last = pe.matmul(dense[0][:, j // 4, :], x[:, par, kc, :], wt[:, s, kk * 512:(kk + 1) * 512],
                                             start=(kc == 0 and x is xt_hi and wt is w_hi), stop=(kc == KC - 1 and x is xt_lo))
                    last.then_inc(S["unit_done"], 1)
                need(pe, S["yb_ready"], e + 1)
                for j in range(4):
                    down(w, j0 + 8 + j, j, 1 - par, e)
                    if j == 2:
                        pe.wait_ge(S["u_free"], e + 2)
                        need(pe, S["at_ready"], e + 1)
                        for c in range(4):
                            last = pe.transpose(duo[:, 0, c * P:(c + 1) * P], ab[:, c * P:(c + 1) * P], ident)
                        last.then_inc(S["bat_done"], 1)

            def down(w, ju, j, par, e):
                pe.wait_ge(S["w_ready"], w.u + ju + 1)
                if j == 0:
                    pe.wait_ge(S["at_ready"], e + 1)
                for x, wt in ((at_hi, w_hi), (at_hi, w_lo), (at_lo, w_hi)):
                    for h in range(2):
                        last = pe.matmul(dense[1][:, h, :], x[:, par, j, :], wt[:, ju % SPLIT, h * 512:(h + 1) * 512],
                                         start=(j == 0 and x is at_hi and wt is w_hi), stop=(j == 3 and x is at_lo))
                last.then_inc(S["unit_done"], 1)

            pe.wait_ge(S["idx_ready"], 1)
            with pe.Fori(0, EXPERTS // 2) as k:
                for par in range(2):
                    expert(k, MOE(k), par)
            pe.wait_ge(S["yb_ready"], EXPERTS + 1)
            for j in range(4):
                down(Part(U_LAST), j, j, 1, EXPERTS)
            pe.wait_ge(S["w_ready"], U_LAST + 8)
            pe.drain().then_inc(S["unit_done"], 4)
            pe.wait_ge(S["yb_ready"], EXPERTS + 2)
            pe.wait_ge(S["xt_ready"], EXPERTS + 1)
            extra = pe.value_load(eint[0:1, EXTRA:EXTRA + 1])
            with pe.Fori(0, EXTRA) as b:
                with pe.If(extra > b):
                    pe.wait_ge(S["bx_in"], b * 16 + 16)
                    for c in range(KC):
                        last = pe.transpose(pair[:, c // 4, (c % 4) * P:(c % 4 + 1) * P], xg[:, 0, c * P:(c + 1) * P], ident)
                    last.then_inc(S["bx_done"], 1)
                    pe.wait_ge(S["bx_ready"], b + 1)
                    pe.wait_ge(S["bw_in"], b * 48 + 48)
                    for h, wt in enumerate((bg, bu)):
                        for kc in range(KC):
                            last = pe.matmul(dense[0][:, h, :], bx[:, kc, :], wt[:, kc // 2, (kc % 2) * 512:(kc % 2 + 1) * 512],
                                             start=(kc == 0), stop=(kc == KC - 1))
                    last.then_inc(S["bgu_done"], 1)
                    pe.wait_ge(S["ba_ready"], b + 1)
                    for c in range(4):
                        last = pe.transpose(duo[:, 0, c * P:(c + 1) * P], ab[:, c * P:(c + 1) * P], ident)
                    last.then_inc(S["bs_done"], 1)
                    pe.wait_ge(S["bat_ready"], b + 1)
                    for h in range(2):
                        for c in range(4):
                            last = pe.matmul(dense[1][:, h, :], ba[:, c, :], bd[:, c, h * 512:(h + 1) * 512],
                                             start=(c == 0), stop=(c == 3))
                    last.then_inc(S["bd_done"], 1)
            for t in range(NT):
                pe.wait_ge(S["o2_ready"], t + 1)
                need(pe, S["x2_ready"], t - 1)
                for c in range(KC):
                    last = pe.transpose(dense[t % 2][:, c // 4, (c % 4) * P:(c % 4 + 1) * P], ot2[:, t % 2, c * P:(c + 1) * P], ident)
                last.then_inc(S["o2_done"], 1)
            sums(KC, 3 * KC, mean, lambda c: rsq[:, c % 2, :], whole)
            barrier(pe, 2)
            barrier(pe, 3)

            cmean = c2[:, D_MEAN:D_MEAN + P]
            rotm = c2[:, D_ROT:D_ROT + P]
            sqs = lambda c: sq2[:, c % 2, :]
            with pe.Fori(0, LAYERS) as l:
                w = LAYER(l)
                n0 = 4 * KC + l * SQS
                fed0 = 32 + l * FEED
                use = lambda d: 32 + l * USES + d // 2
                sums(KC, n0, cmean, sqs, halves)
                for j in range(5):
                    dense_unit(w, j, use(j), j % 2, halves, x_hi, x_lo, fed0 if j == 0 else None)
                    need(pe, dense_free[j % 2], use(j) + 1)
                    need(pe, S["rot_used"], l * 5 + j + 1)
                    src = qb[:, j, :] if j < 4 else kb[:, :]
                    for h, (t0, n) in enumerate(halves):
                        last = pe.matmul(pair[:, h, 0:n], rotm, src[:, t0:t0 + n], start=True, stop=True)
                    last.then_inc(S["rot_done"], 1)
                need(pe, S["w_ready"], w.u + 6)
                need(pe, dense_free[1], use(5))
                for t in range(QB):
                    t0, n = (0, META) if t == 0 else (META + P * (t - 1), P)
                    for kc in range(KC):
                        for x, wt in ((x_hi, w_hi), (x_hi, w_lo), (x_lo, w_hi)):
                            last = pe.matmul(dense[1][0:n, t // 4, (t % 4) * P:(t % 4 + 1) * P], x[:, kc, t0:t0 + n],
                                             wt[:, 5 % SPLIT, kc * P:(kc + 1) * P],
                                             start=(kc == 0 and x is x_hi and wt is w_hi), stop=(kc == KC - 1 and x is x_lo))
                last.then_inc(S["unit_done"], 1)
                need(pe, dense_free[1], use(5) + 1)
                pe.wait_ge(S["kv_ready"], l * 5 + 5 + 1)

                def narrow_need(n, sem, value):
                    if n == 0:
                        value = pe.to_reg(value)
                        pe.wait_ge(S["const_in"], 32)
                    need(pe, sem, value)

                def transposes(i, hp):
                    n, g, q0, nq, keys = item(i)
                    if hp == 0:
                        pe.wait_ge(S["ex_done"], l * 10 + i + 1)
                    narrow_need(n, S["pt_free"], l * PTS + ptseq(i, hp) + 1)
                    k0 = 0
                    for kt, (_, _, nk) in enumerate(keys):
                        for h in range(2):
                            o = (2 * kt + h) * P
                            last = pe.transpose(pair[0:nk, 1, o:o + nq], sc[0:nq, i % 2, 2 * hp + h, k0:k0 + nk], c2[0:nq, D_IDENT:D_IDENT + nq])
                        k0 += nk
                    last.then_inc(S["pt_done"], 1)

                for s in range(STEPS):
                    if s < 10:
                        n, g, q0, nq, keys = item(s)
                        narrow_need(n, S["mk_ready"], l * 10 + s + 1)
                        k0, nk = keys[0][1], sum(x[2] for x in keys)
                        for h in range(4):
                            r = slice(g * HD, (g + 1) * HD)
                            last = pe.matmul(duo[0:nq, h // 2, (h % 2) * 256:(h % 2) * 256 + nk], qb[r, h, q0:q0 + nq],
                                             kb[r, k0:k0 + nk], start=True, stop=True)
                        last.then_inc(S["sc_done"], 1)
                    if s >= 5 and s % 2 == 1:
                        n = (s - 5) // 2
                        nq = META if n == 0 else P
                        pe.wait_ge(S["o_ready"], l * QB + n + 1)
                        narrow_need(n, S["pt_free"], l * PTS + atseq(n) + 1)
                        for c in range(4):
                            last = pe.transpose(pair[:, 1, c * P:c * P + nq],
                                                ot[0:nq, n % 2, 2 * c:2 * c + 2, :].rearrange("p h d -> p (h d)"), c2[0:nq, D_IDENT:D_IDENT + nq])
                        last.then_inc(S["pt_done"], 1)
                    if 0 <= s - 1 < 10:
                        transposes(s - 1, 0)
                    if s < 12:
                        j = 6 + s
                        dense_unit(w, j, use(j), j % 2, halves, x_hi, x_lo)
                    if 0 <= s - 1 < 10:
                        transposes(s - 1, 1)
                    if 0 <= s - 2 < 10:
                        i = s - 2
                        n, g, q0, nq, keys = item(i)
                        narrow_need(n, S["at2_ready"], l * 10 + i + 1)
                        narrow_need(n, S["pt_free"], l * PTS + ptseq(i, 1) + 2)
                        for h in range(4):
                            for kt, (tile, _, nk) in enumerate(keys):
                                last = pe.matmul(pair[0:nq, 0, h * HD:(h + 1) * HD], pt[0:nk, i % 2, kt, h, 0:nq],
                                                 vb[0:nk, tile, g * HD:(g + 1) * HD], start=(kt == 0), stop=(kt == len(keys) - 1))
                        last.then_inc(S["pv_done"], 1)
                pe.wait_ge(S["pt_free"], l * PTS + PTS + 1)
                sums(4, n0 + 8, c2[:, D_MEAN2:D_MEAN2 + P], sqs, halves)
                for j in range(L_OUT, L_MLP):
                    dense_unit(w, j, use(j), j % 2, halves, x_hi, x_lo, fed0 + 8 if j == L_OUT else None)
                    if j > L_OUT:
                        sums(KC, n0 + 12, cmean, sqs, halves, only=[j - L_OUT - 1])
                sums(KC, n0 + 12, cmean, sqs, halves, only=[KC - 1])
                sums(KC, n0 + 20, cmean, sqs, halves)
                with pe.Fori(0, QUARTERS) as q:
                    wq = LAYER(l, q)
                    useq = lambda d: 32 + l * USES + q * 8 + d // 2
                    for m in range(8):
                        j = L_MLP + m
                        dense_unit(wq, j, useq(j), j % 2, halves, x_hi, x_lo, fed0 + 16 if m == 0 else None)
                    for m in range(8):
                        j = L_MLP + 8 + m
                        dense_unit(wq, j, useq(j), j % 2, halves, k_hi, k_lo, fed0 + 24 + q * 8 if m == 0 else None)
                for n in range(L_DUMMY, PER_LAYER, SPLIT):
                    n1 = min(n + SPLIT, PER_LAYER)
                    pe.wait_ge(S["w_ready"], w.u + n1)
                    pe.drain().then_inc(S["unit_done"], n1 - n)
                sums(KC, n0 + 28, cmean, sqs, halves)

        @block.scalar
        def _(act):
            for name in ("silu_done", "yb_ready"):
                act.drain().then_inc(S[name], FROM[name])

            def tick(w, j):
                v = j + AHEAD
                act.wait_ge(raw_in[v % RAW // 2], (w.u8 + v // RAW) * 16 + 16)
                need(act, S["unit_done"], w.u + v - SPLIT + 1)
                act.activation(w_hi[:, v % SPLIT, :], raw[:, v % RAW, :], ACT.Copy).then_inc(S["hi_done"], 1)

            def high(src, dst, ready=None):
                if ready is not None:
                    act.wait_ge(S["val_ready"], ready)
                act.activation(dst, src, ACT.Copy).then_inc(S["xh_done"], 1)

            def square(n, dst, src, extra=()):
                need(act, S["sq_used"], n - 1)
                act.activation(dst, src, ACT.Square).then_inc(S["sq_ready"], 1)

            def root(n, out, src):
                act.wait_ge(S["sq_used"], n)
                act.activation(out, src, ACT.Sqrt, bias=consts[:, C_EPS:C_EPS + 1]).then_inc(S["root_ready"], 1)

            def evac(u, which, out, func, bias=0.0):
                act.wait_ge(S["unit_done"], u + 1)
                return act.activation(out, dense[which][:, 0, :], func, bias=bias)

            for j in range(-AHEAD, 0):
                tick(Part(0), j)
            act.wait_ge(S["x_in"], 16)
            act.wait_ge(S["const_in"], 32)
            for c in range(KC):
                square(c, sq[:, c % 2, :], stage[:, c, :])
            root(KC, rstd[:, :], pair[:, 0, :])
            for c in range(KC):
                high(val[:, c % 3, :], x_hi[:, c, 0:T], c + 1)
            for m in range(8):
                tick(Part(U_A2), m)
                d = m
                evac(U_A2 + m, d % 2, stage[:, m, :], ACT.Sigmoid, col("b_in", 8 + m)).then_inc(dense_free[d % 2], 1)
            for m in range(8):
                tick(Part(U_A1), m)
            for j in range(8):
                tick(Part(U_V), j)
                if j % 4 == 3:
                    for t in range(NT):
                        k = NT * (j // 4) + t
                        act.wait_ge(S["v_sum"], k + 1)
                        v = vtok[:, t, (j // 4) * 512:(j // 4 + 1) * 512]
                        act.activation(v, v, ACT.Gelu).then_inc(S["v_gelu"], 1)
            for m in range(8):
                tick(Part(U_U), m)
                if m == 0:
                    act.wait_ge(S["ms_ready"], 1)
                    act.activation(vrs[:, :], vmv[:, :, 1], ACT.Sqrt, bias=consts[:, C_EPS:C_EPS + 1]).then_inc(S["root_ready"], 1)
                d = U_U - 8 + m
                ins = evac(U_U + m, d % 2, ubuf[:, m, :], ACT.Gelu, col("b_in", 16 + m))
                ins.then_inc(dense_free[d % 2], 1)
            for m in range(8):
                tick(Part(U_GA), m)
                d = U_GA - 8 + m
                if m == 0:
                    act.wait_ge(S["v_sum"], 8)
                evac(U_GA + m, d % 2, gate_a[:, m, :], ACT.Sigmoid, col("b_in", 32 + m)).then_inc(dense_free[d % 2], 1)
            for m in range(8):
                tick(Part(U_GB), m)
                d = U_GB - 8 + m
                if m == 0:
                    act.wait_ge(S["sp_done"], HEADS_SG)
                evac(U_GB + m, d % 2, stage[:, m, :], ACT.Sigmoid, col("b_in", 40 + m)).then_inc(dense_free[d % 2], 1)
            act.wait_ge(S["unit_done"], U_SGO)
            for c in range(KC):
                high(ubuf[:, c, :], x_hi[:, c, 0:T], KC + c + 1)
            for m in range(8):
                tick(Part(U_SGO), m)
                if m == 2:
                    for c in range(KC):
                        act.wait_ge(S["yc_ready"], c + 1)
                        square(KC + c, sq[:, c % 2, :], y1[:, c, :])
                if m == 6:
                    root(2 * KC, rstd[:, :], pair[:, 0, :])
                    for c in range(KC):
                        act.wait_ge(S["t_ready"], c + 1)
                        act.activation(y1[:, c, :], y1[:, c, :], ACT.Silu, bias=col("conv_ln_b", c),
                                       scale=col("conv_ln_g", c)).then_inc(S["val_ready"], 1)
            act.wait_ge(S["unit_done"], U_CVO)
            for c in range(KC):
                high(y1[:, c, :], x_hi[:, c, 0:T], 2 * KC + c + 1)
            for m in range(8):
                tick(Part(U_CVO), m)
            act.wait_ge(S["unit_done"], U_OUT)
            for c in range(KC):
                high(gate_a[:, c, :], x_hi[:, c, 0:T], 3 * KC + c + 1)
            for m in range(8):
                tick(Part(U_OUT), m)
            barrier(act, 1)

            for c in range(KC):
                square(2 * KC + c, rsq[:, c % 2, :], y1[:, c, :])
            root(3 * KC, rrs[:, :], pair[:, 0, :])
            for t in range(NT):
                act.wait_ge(S["tr_done"], t + 1)
                act.activation(htok[:, t, :], dense[t % 2][:, :, :].rearrange("p a b -> p (a b)"), ACT.Copy).then_inc(S["ht_ready"], 1)
                act.wait_ge(S["ht_ready"], t + 1)
                act.dma_start(hrows[t * P:(t + 1) * P, :], htok[:, t, :]).then_inc(S["hrows_in"], 16)
            act.wait_ge(S["gx_ready"], 1)
            act.activation(rt[:, 10, :, 0:GROUPS], rt[:, 10, :, 0:GROUPS], ACT.Exp).then_inc(S["ge_ready"], 1)
            act.wait_ge(S["gx_ready"], 2)
            act.activation(rs[:, 20, :], rs[:, 20, :], ACT.Exp).then_inc(S["ge_ready"], 1)

            def columns(e, par):
                act.wait_ge(S["xt_done"], e + 1)
                act.activation(xt_hi[:, par, :, :].rearrange("p c t -> p (c t)"),
                               pair[:, :, :].rearrange("p a b -> p (a b)"), ACT.Copy).then_inc(S["xth_done"], 1)

            def results(done, par, scattered):
                act.wait_ge(S["unit_done"], done)
                need(act, ys_out[par], scattered)
                act.activation(yb[:, par, :], dense[1][:, :, :].rearrange("p a b -> p (a b)"), ACT.Copy).then_inc(S["yb_ready"], 1)

            columns(0, 0)

            def expert(k, w, par, before):
                e = 2 * k + par
                j0 = PER_EXPERT * par
                for j in range(PER_EXPERT):
                    tick(w, j0 + j)
                    if j == 0 and before:
                        results(w.u + j0, 1 - par, 16 * (k - 1))
                    if j == 4:
                        act.wait_ge(S["unit_done"], w.u + j0 + 4)
                        need(act, S["u_free"], e + 1)
                        act.activation(gs[:, :], dense[0][:, 0, :], ACT.Silu).then_inc(S["silu_done"], 1)
                    if j == 5:
                        columns(e + 1, 1 - par)
                    if j == 11:
                        act.wait_ge(S["bat_done"], e + 1)
                        act.activation(at_hi[:, par, :, :].rearrange("p c t -> p (c t)"), duo[:, 0, :], ACT.Copy).then_inc(S["ath_done"], 1)

            for k in range(2):
                expert(k, MOE(k), 0, k > 0)
                expert(k, MOE(k), 1, True)
            with act.Fori(2, EXPERTS // 2) as k:
                expert(k, MOE(k), 0, True)
                expert(k, MOE(k), 1, True)
            tick(Part(U_LAST), 0)
            results(U_LAST, 1, 16 * (EXPERTS // 2 - 1))
            for j in range(1, 8):
                tick(Part(U_LAST), j)
                if j == 4:
                    results(U_LAST + 4, 0, 16 * (EXPERTS // 2 - 1))
            act.wait_ge(ys_out[0], 16 * EXPERTS // 2)
            extra = act.value_load(eint[0:1, EXTRA:EXTRA + 1])
            with act.Fori(0, EXTRA) as b:
                with act.If(extra > b):
                    e = act.value_load(eint[0:1, bass.ds(b, 1)], min_val=0, max_val=EXPERTS - 1)
                    for dst, u in ((bg, 0), (bu, 4), (bd, 2 * PER_EXPERT - 4)):
                        act.dma_start(dst[:, :, :], W[bass.ds(e * PER_EXPERT + U_MOE + u, 4)].rearrange("u p n -> p u n")
                                      ).then_inc(S["bw_in"], 16)
                    act.wait_ge(S["bx_done"], b + 1)
                    act.activation(bx[:, :, :].rearrange("p c t -> p (c t)"), pair[:, :, :].rearrange("p a b -> p (a b)"), ACT.Copy).then_inc(S["bx_ready"], 1)
                    act.wait_ge(S["bgu_done"], b + 1)
                    act.activation(gs[:, :], dense[0][:, 0, :], ACT.Silu).then_inc(S["bg_ready"], 1)
                    act.wait_ge(S["bs_done"], b + 1)
                    act.activation(ba[:, :, :].rearrange("p c t -> p (c t)"), duo[:, 0, :], ACT.Copy).then_inc(S["bat_ready"], 1)
                    act.wait_ge(S["bd_done"], b + 1)
                    act.activation(yb[:, 0, :], dense[1][:, :, :].rearrange("p a b -> p (a b)"), ACT.Copy).then_inc(S["by_ready"], 1)
            for c in range(KC):
                act.wait_ge(S["x2_ready"], NT)
                square(3 * KC + c, rsq[:, c % 2, :], y1[:, c, :])
            root(4 * KC, rrs[:, :], pair[:, 0, :])
            barrier(act, 2)
            barrier(act, 3)

            def two(ap):
                return ap.rearrange("p (h t) -> p h t", h=2)

            with act.Fori(0, LAYERS) as l:
                w = LAYER(l)
                n0 = 4 * KC + l * SQS
                v0 = 4 * KC + l * VALS
                used = lambda d: 32 + l * USES + d // 2

                def root2(n):
                    act.wait_ge(S["sq_used"], n)
                    act.activation(two(rstd2[:, :]), pair[:, :, 0:HALF], ACT.Sqrt, bias=c2[:, D_EPS:D_EPS + 1]
                                   ).then_inc(S["root_ready"], 1)

                def copy_out(w, j, out, func=ACT.Copy):
                    act.wait_ge(S["unit_done"], w.u + j + 1)
                    act.activation(two(out), dense[j % 2][:, :, 0:HALF], func).then_inc(dense_free[j % 2], 1)

                act.wait_ge(S["fr_done"], l * 8 + 1)
                for c in range(KC):
                    square(n0 + c, sq2[:, c % 2, :], res[:, c, :])
                root2(n0 + 8)
                for c in range(KC):
                    high(val2[:, c % 3, :], x_hi[:, c, :], v0 + c + 1)
                for j in range(5):
                    tick(w, j)
                    copy_out(w, j, qb[:, j, :] if j < 4 else kb[:, :])
                tick(w, 5)
                act.wait_ge(S["unit_done"], w.u + 6)
                act.activation(vb[0:META, 0, :], dense[1][0:META, 0, 0:P], ACT.Copy)
                act.activation(vb[:, 1:4, :], dense[1][:, 0, P:4 * P].rearrange("p (t c) -> p t c", t=3), ACT.Copy)
                act.activation(vb[:, 4, :], dense[1][:, 1, 0:P], ACT.Copy).then_inc(dense_free[1], 1)

                def weights_out(i, hp):
                    n, g, q0, nq, keys = item(i)
                    act.wait_ge(S["pt_done"], l * PTS + ptseq(i, hp) + 1)
                    if i:
                        need(act, S["pv_done"], l * 10 + i)
                    for kt, (_, _, nk) in enumerate(keys):
                        last = act.activation(pt[0:nk, i % 2, kt, 2 * hp:2 * hp + 2, 0:nq],
                                              pair[0:nk, 1, 2 * kt * P:(2 * kt + 2) * P].rearrange("p (h t) -> p h t", h=2)[:, :, 0:nq],
                                              ACT.Copy)
                    last.then_inc(S["pt_free"], 1)

                for s in range(STEPS):
                    if s < 12:
                        tick(w, 6 + s)
                    if 0 <= s - 1 < 10:
                        weights_out(s - 1, 0)
                    if s < 10:
                        n, g, q0, nq, keys = item(s)
                        nk = sum(x[2] for x in keys)
                        act.wait_ge(S["mk_ready"], l * 10 + s + 2)
                        for h in range(4):
                            row = sc[0:nq, s % 2, h, 0:nk]
                            act.activation(row, row, ACT.Exp, bias=sm[0:nq, s % 4, 1, h:h + 1], accum_out=sm[0:nq, s % 4, 3, h:h + 1])
                        act.activation(sm[0:nq, s % 4, 2, :], sm[0:nq, s % 4, 2, :], ACT.Exp).then_inc(S["ex_done"], 1)
                    if s < 8:
                        copy_out(w, 6 + s, (bb if s < 4 else cb)[:, s % 4, :])
                    if 0 <= s - 1 < 10:
                        weights_out(s - 1, 1)
                    if s >= 4 and s % 2 == 0:
                        n = (s - 4) // 2
                        nq = META if n == 0 else P
                        act.wait_ge(S["om_ready"], l * QB + n + 2)
                        act.activation(orr[0:nq, 1:2], orr[0:nq, 0:1], ACT.Sqrt, bias=c2[0:nq, D_EPS:D_EPS + 1], scale=1.0 / 512
                                       ).then_inc(S["os_ready"], 1)
                for c in range(4):
                    act.wait_ge(S["cv_ready"], l * 4 + c + 1)
                    square(n0 + 8 + c, sq2[:, c % 2, :], cb[:, c, :])
                root2(n0 + 12)
                act.wait_ge(S["pt_free"], l * PTS + PTS + 1)
                act.wait_ge(S["unit_done"], w.u + L_OUT)
                for c in range(4):
                    high(yat[:, c, :], x_hi[:, c, :])
                for c in range(4):
                    high(cb[:, c, :], x_hi[:, 4 + c, :], v0 + 8 + c + 1)
                for m in range(8):
                    j = L_OUT + m
                    tick(w, j)
                    copy_out(w, j, fb[:, m, :])
                    act.wait_ge(dense_free[j % 2], used(j) + 1)
                    square(n0 + 12 + m, sq2[:, m % 2, :], fb[:, m, :])
                root2(n0 + 20)
                for c in range(KC):
                    act.wait_ge(S["res_ready"], l * 8 + c + 1)
                    square(n0 + 20 + c, sq2[:, c % 2, :], res[:, c, :])
                root2(n0 + 28)
                act.wait_ge(S["unit_done"], w.u + L_MLP)
                for c in range(KC):
                    high(val2[:, c % 3, :], x_hi[:, c, :], v0 + 12 + c + 1)
                with act.Fori(0, QUARTERS) as q:
                    wq = LAYER(l, q)
                    vq = v0 + 20 + q * 8
                    for m in range(8):
                        tick(wq, L_MLP + m)
                        if m:
                            if m == 1:
                                act.wait_ge(S["unit_done"], wq.u + L_MLP)
                            high(val2[:, (m - 1) % 3, :], k_hi[:, m - 1, :], vq + m)
                            if m >= 2:
                                act.wait_ge(S["val_ready"], vq + m - 1)
                        copy_out(wq, L_MLP + m, rl[:, m % 2, :], ACT.Relu)
                    high(val2[:, 7 % 3, :], k_hi[:, 7, :], vq + 8)
                    for m in range(8):
                        tick(wq, L_MLP + 8 + m)
                for j in range(L_DUMMY, PER_LAYER):
                    tick(w, j)
                for c in range(KC):
                    act.wait_ge(dense_free[c % 2], used(48 + L_MLP + 8 + c) + 1)
                    square(n0 + 28 + c, sq2[:, c % 2, :], fb[:, c, :])
                root2(n0 + 36)

        @block.vector
        def _(dve):
            dc = Count(dve, S["dve_chain"])
            for name in ("u_free", "rot_used", "kv_ready", "pt_free", "mk_ready", "at2_ready", "om_ready"):
                dve.engine_nop().then_inc(S[name], FROM[name])

            def step(ins):
                dc.add(ins)
                dc.wait()

            def tick(w, j):
                v = j + AHEAD
                dve.wait_ge(S["hi_done"], w.u + v + 1)
                dve.tensor_tensor(w_lo[:, v % SPLIT, :], raw[:, v % RAW, :], w_hi[:, v % SPLIT, :].bitcast(F32),
                                  ALU.subtract).then_inc(S["w_ready"], 1)

            def low_part(n, src, hi, lo):
                dve.wait_ge(S["xh_done"], n)
                dve.tensor_tensor(lo, src, hi.bitcast(F32), ALU.subtract).then_inc(S["x_ready"], 1)

            def inverse(k, r):
                dve.wait_ge(S["root_ready"], k)
                step(dve.reciprocal(r, r))

            def scaled(out, x, gain, r):
                return dve.scalar_tensor_tensor(out, x, gain, r, ALU.mult, ALU.mult)

            for j in range(-AHEAD, 0):
                tick(Part(0), j)
            dve.wait_ge(S["const_in"], 32)
            dve.wait_ge(S["x_in"], 16)
            inverse(1, rstd[:, :])

            def feed_normed(n0, vals, xs, gain, r, hi, lo, width):
                for c in range(KC + 1):
                    if c < KC:
                        if c >= 3:
                            dve.wait_ge(S["x_ready"], n0 + c - 2)
                        scaled(vals[:, c % 3, :], xs[:, c, :], gain(c), r).then_inc(S["val_ready"], 1)
                    if c:
                        low_part(n0 + c, vals[:, (c - 1) % 3, :], hi[:, c - 1, 0:width], lo[:, c - 1, 0:width])

            feed_normed(0, val, stage, lambda c: col("norm_mix_g", c), rstd[:, :], x_hi, x_lo, T)

            taps = [(c, k) for c0 in range(0, DVE_CONV, 2) for k in range(TAPS) for c in (c0, c0 + 1)]
            done = [0]

            def convolve(n):
                for c, k in taps[done[0]:done[0] + n]:
                    if done[0] >= 2:
                        dve.wait_ge(S["conv_done"], done[0] - 1)
                    wc = col("conv_w", c * TAPS + k)
                    if k == 0:
                        ins = dve.tensor_scalar(y1[:, c, :], apad[:, c, 0:T], wc, col("conv_b", c), ALU.mult, ALU.add)
                    else:
                        ins = dve.scalar_tensor_tensor(y1[:, c, :], apad[:, c, k:k + T], wc, y1[:, c, :], ALU.mult, ALU.add)
                    ins.then_inc(S["conv_done"], 1)
                    done[0] += 1

            def gated(u, d, out, bias, gate):
                dve.wait_ge(S["unit_done"], u + 1)
                return dve.scalar_tensor_tensor(out, dense[d % 2][:, 0, :], bias, gate, ALU.add, ALU.mult)

            for m in range(8):
                tick(Part(U_A2), m)
            dve.wait_ge(S["pool_chain"], 1)
            for m in range(8):
                tick(Part(U_A1), m)
                d = U_A1 + m
                dve.wait_ge(dense_free[m % 2], m // 2 + 1)
                gated(U_A1 + m, d, apad[:, m, PAD:], col("b_in", m), stage[:, m, :]).then_inc(dense_free[d % 2], 1)
                dve.wait_ge(dense_free[d % 2], d // 2 + 1)
                if m >= 2:
                    convolve(TAPS_PER_STEP)
            dve.wait_ge(S["aux_in"], 48)

            def v_bias(h):
                for t in range(NT):
                    bank = (dense[0], dense[1], pair, duo)[2 * h + t // 2][:, t % 2, :]
                    dve.tensor_tensor(vtok[:, t, h * 512:(h + 1) * 512], bank, bv_sb[:, h * 512:(h + 1) * 512], ALU.add
                                      ).then_inc(S["v_sum"], 1)

            def v_stats(h):
                for t in range(NT):
                    dve.wait_ge(S["v_gelu"], NT * h + t + 1)
                    dc.add(dve.bn_stats(vst[:, t, h, :], vtok[:, t, h * 512:(h + 1) * 512]))

            for j in range(8):
                tick(Part(U_V), j)
                if j == 3:
                    dve.wait_ge(S["unit_done"], U_V + 4)
                    v_bias(0)
                if j == 7:
                    dve.wait_ge(S["unit_done"], U_V + 8)
                    v_bias(1)
                convolve(TAPS_PER_STEP)
                if j == 5:
                    v_stats(0)
            for m in range(8):
                tick(Part(U_U), m)
                if m == 0:
                    v_stats(1)
                    dc.wait()
                    for t in range(NT):
                        dc.add(dve.bn_aggr(vmv[:, t, :], vst[:, t, :, :].rearrange("p a b -> p (a b)")))
                    dc.wait()
                    dve.engine_nop().then_inc(S["ms_ready"], 1)
                    inverse(2, vrs[:, :])
                    for t in range(NT):
                        dve.tensor_scalar(vtok[:, t, :], vtok[:, t, :], vmv[:, t, 0:1], vrs[:, t:t + 1],
                                          ALU.subtract, ALU.mult).then_inc(S["vn_ready"], 1)
                convolve(TAPS_PER_STEP)
            for m in range(8):
                tick(Part(U_GA), m)
                if m == 0:
                    dve.wait_ge(S["rows_done"], 1)
                    for h in range(HEADS_SG):
                        dc.add(dve.scalar_tensor_tensor(bs_sb[:, h, :], pair[:, h // 4, (h % 4) * P:(h % 4 + 1) * P],
                                                        col("sg_ln_b", h), bs_sb[:, h, :], ALU.mult, ALU.add))
                    dc.wait()
                convolve(TAPS_PER_STEP)
                dve.wait_ge(S["sp_done"], m + 1)
                dve.wait_ge(S["x_ready"], KC)
                if m >= 2:
                    dve.wait_ge(S["val_ready"], KC + m - 1)
                need(dve, dense_free[m % 2], (U_U - 8 + m) // 2 + 1)
                blocks = val[:, m % 2, :].rearrange("p (n q) -> p n q", n=NT)
                dve.scalar_tensor_tensor(blocks, duo[:, m % 2, :].rearrange("p (n q) -> p n q", n=NT), col("sg_ln_g", m),
                                         bs_sb[:, m, :].unsqueeze(1).broadcast_to([P, NT, P]), ALU.mult, ALU.add
                                         ).then_inc(S["sp_free"], 1)
                dve.wait_ge(S["sp_free"], m + 1)
                dve.tensor_tensor(ubuf[:, m, :], val[:, m % 2, :], ubuf[:, m, :], ALU.mult).then_inc(S["val_ready"], 1)
            for m in range(8):
                tick(Part(U_GB), m)
                convolve(TAPS_PER_STEP)
            convolve(len(taps))
            for c in range(KC):
                low_part(KC + c + 1, ubuf[:, c, :], x_hi[:, c, 0:T], x_lo[:, c, 0:T])
            for m in range(8):
                tick(Part(U_SGO), m)
                d = U_SGO - 8 + m
                if m == 2:
                    dve.wait_ge(S["s1_done"], KC)
                    step(dve.tensor_copy(mu[:, :], pair[:, 0, :]))
                    for c in range(KC):
                        dve.tensor_tensor(y1[:, c, :], y1[:, c, :], mu[:, :], ALU.subtract).then_inc(S["yc_ready"], 1)
                if m == 6:
                    inverse(3, rstd[:, :])
                    for c in range(KC):
                        dve.tensor_tensor(y1[:, c, :], y1[:, c, :], rstd[:, :], ALU.mult).then_inc(S["t_ready"], 1)
                need(dve, dense_free[m % 2], (U_GB - 8 + m) // 2 + 1)
                gated(U_SGO + m, d, stage[:, m, :], col("b_sg_out", m), stage[:, m, :]).then_inc(dense_free[d % 2], 1)
            for c in range(KC):
                low_part(2 * KC + c + 1, y1[:, c, :], x_hi[:, c, 0:T], x_lo[:, c, 0:T])
            for m in range(8):
                tick(Part(U_CVO), m)
                d = U_CVO - 8 + m
                gated(U_CVO + m, d, gate_a[:, m, :], col("b_conv_out", m), gate_a[:, m, :]).then_inc(dense_free[d % 2], 1)
                dve.wait_ge(dense_free[d % 2], d // 2 + 1)
                dve.tensor_tensor(gate_a[:, m, :], gate_a[:, m, :], stage[:, m, :], ALU.add).then_inc(S["val_ready"], 1)
            for c in range(KC):
                low_part(3 * KC + c + 1, gate_a[:, c, :], x_hi[:, c, 0:T], x_lo[:, c, 0:T])
            dve.wait_ge(S["xr_in"], 16)
            for m in range(8):
                tick(Part(U_OUT), m)
                d = U_OUT - 8 + m
                dve.wait_ge(S["unit_done"], U_OUT + m + 1)
                dve.scalar_tensor_tensor(y1[:, m, :], dense[d % 2][:, 0, :], col("b_out", m), xr[:, m, :], ALU.add, ALU.add
                                         ).then_inc(dense_free[d % 2], 1)
            barrier(dve, 1)

            dve.memset(at_hi[:, 1, :, :].bitcast(F32), 0.0)
            dve.memset(at_lo[:, 1, :, :].bitcast(F32), 0.0).then_inc(S["at_ready"], 1)
            inverse(4, rrs[:, :])
            for c in range(KC):
                scaled(hb[:, c, :], y1[:, c, :], col("norm_ffn_g", c), rrs[:, :]).then_inc(S["hb_ready"], 1)
            tt, ts, stt, red = dve.tensor_tensor, dve.tensor_scalar, dve.scalar_tensor_tensor, dve.tensor_reduce
            R = lambda i: rs[:, i, :]
            iota = lambda n: consts[:, C_IOTA:C_IOTA + n]
            wide = lambda ap, n: ap.unsqueeze(2).broadcast_to([P, NT, n])
            over = lambda ap, n: ap.unsqueeze(1).broadcast_to([P, NT, n])
            G, E = lg[:, :, 0:GROUPS], lg[:, :, GROUPS:ROUTER]

            def first_max(x, n, best, index):
                step(red(R(best), x, AX_X, ALU.max))
                step(tt(rt[:, 0, :, 0:n], x, wide(R(best), n), ALU.is_equal))
                step(stt(rt[:, 1, :, 0:n], rt[:, 0, :, 0:n], -64.0, over(iota(n), n), ALU.mult, ALU.add))
                step(red(R(index), rt[:, 1, :, 0:n], AX_X, ALU.min))
                step(ts(R(index), R(index), 64.0, None, ALU.add))

            dve.wait_ge(S["lg_done"], 1)
            dve.wait_ge(S["mask_in"], 32)
            step(tt(lg[:, :, :], duo[:, 0, 0:NT * ROUTER].rearrange("p (t r) -> p t r", t=NT), over(rb_sb[:, :], ROUTER), ALU.add))
            first_max(G, GROUPS, 0, 1)
            tt(rt[:, 10, :, 0:GROUPS], G, wide(R(0), GROUPS), ALU.subtract).then_inc(S["gx_ready"], 1)
            step(tt(rt[:, 4, :, 0:GROUPS], over(iota(GROUPS), GROUPS), wide(R(1), GROUPS), ALU.is_equal))
            spread = rt[:, 0, :, :].rearrange("p t (g e) -> p t g e", g=GROUPS)
            step(tt(spread, E.rearrange("p t (g e) -> p t g e", g=GROUPS),
                    rt[:, 4, :, 0:GROUPS].unsqueeze(3).broadcast_to([P, NT, GROUPS, PER_GROUP]), ALU.mult))
            step(red(rt[:, 5, :, 0:PER_GROUP], spread.rearrange("p t g e -> p t e g"), AX_X, ALU.add))
            el = rt[:, 5, :, 0:PER_GROUP]
            first_max(el, PER_GROUP, 4, 5)
            step(tt(rt[:, 1, :, 0:PER_GROUP], over(iota(PER_GROUP), PER_GROUP), wide(R(5), PER_GROUP), ALU.is_equal))
            step(stt(rt[:, 11, :, 0:PER_GROUP], rt[:, 1, :, 0:PER_GROUP], -3.0e38, el, ALU.mult, ALU.add))
            first_max(rt[:, 11, :, 0:PER_GROUP], PER_GROUP, 6, 7)
            tt(R(20), R(6), R(4), ALU.subtract).then_inc(S["gx_ready"], 1)
            for j in range(2):
                step(stt(R(8 + j), R(1), float(PER_GROUP), R(5 + 2 * j), ALU.mult, ALU.add))
                step(tt(rt[:, 2 + j, :, :], over(iota(EXPERTS), EXPERTS), wide(R(8 + j), EXPERTS), ALU.is_equal))
            tt(rt[:, 6, :, :], rt[:, 2, :, :], rt[:, 3, :, :], ALU.add).then_inc(S["rank_ready"], 1)
            dve.wait_ge(S["ge_ready"], 2)
            step(red(R(2), rt[:, 10, :, 0:GROUPS], AX_X, ALU.add))
            step(dve.reciprocal(R(3), R(2)))
            step(ts(R(21), R(20), 1.0, None, ALU.add))
            step(dve.reciprocal(R(22), R(21)))
            step(tt(wts[:, 0, :], R(22), R(3), ALU.mult))
            step(tt(wts[:, 1, :], wts[:, 0, :], R(20), ALU.mult))
            dve.wait_ge(S["rank_done"], 1)
            step(dve.tensor_copy(rt[:, 7, :, :], duo[:, 1, 0:NT * EXPERTS].rearrange("p (t e) -> p t e", t=NT)))
            step(dve.tensor_copy(rt[:, 8, 0, :], duo[:, 1, NT * EXPERTS:(NT + 1) * EXPERTS]))
            counts, more, pa, pb = rt[:, 8, 0, :], rt[:, 8, 1, :], rt[:, 9, 0, :], rt[:, 9, 1, :]
            step(ts(more, counts, float(P), None, ALU.is_gt))
            for k in (2, 3):
                step(stt(more, counts, float(k * P), more, ALU.is_gt, ALU.add))
            step(dve.tensor_copy(pa, more))
            for sh in (1, 2, 4, 8, 16):
                step(dve.tensor_copy(pb[:, 0:sh], pa[:, 0:sh]))
                step(tt(pb[:, sh:], pa[:, sh:], pa[:, 0:EXPERTS - sh], ALU.add))
                pa, pb = pb, pa
            before = rt[:, 9, 2, :]
            step(tt(before, pa, more, ALU.subtract))
            for j in range(2):
                step(tt(rt[:, 0, :, :], rt[:, 7, :, :], rt[:, 2 + j, :, :], ALU.mult))
                step(red(R(10 + j), rt[:, 0, :, :], AX_X, ALU.add))
                step(tt(rt[:, 0, :, :], rt[:, 2 + j, :, :], over(before, EXPERTS), ALU.mult))
                step(red(R(12 + j), rt[:, 0, :, :], AX_X, ALU.add))
                step(ts(R(14 + j), R(10 + j), float(P), None, ALU.is_ge))
                for k in (2, 3):
                    step(stt(R(14 + j), R(10 + j), float(k * P), R(14 + j), ALU.is_ge, ALU.add))
                step(stt(R(16 + j), R(14 + j), -float(P), R(10 + j), ALU.mult, ALU.add))
                step(tt(R(23), R(12 + j), R(14 + j), ALU.add))
                step(stt(R(24), R(23), float(EXPERTS - 1), R(8 + j), ALU.add, ALU.subtract))
                step(stt(R(25), R(14 + j), 0.0, R(24), ALU.is_gt, ALU.mult))
                step(tt(R(18 + j), R(8 + j), R(25), ALU.add))
            cmp = rt[:, 0:2, :, :].rearrange("p a t e -> p (a t) e")[:, 0:EXTRA, :]
            step(tt(cmp, pa.unsqueeze(1).broadcast_to([P, EXTRA, EXPERTS]),
                    iota(EXTRA).unsqueeze(2).broadcast_to([P, EXTRA, EXPERTS]), ALU.is_le))
            step(red(rt[:, 8, 2, 0:EXTRA], cmp, AX_X, ALU.add))
            step(dve.tensor_copy(rt[:, 8, 2, EXTRA:EXTRA + 1], pa[:, EXPERTS - 1:EXPERTS]))
            step(dve.tensor_copy(eint[:, :], rt[:, 8, 2, 0:EXTRA + 1]))
            for k in range(2 * NT):
                j, t = k // NT, k % NT
                need(dve, S["list_done"], k - 1)
                row, blk = rs[:, 16 + j, t:t + 1], rs[:, 18 + j, t:t + 1]
                ts(onr[:, k % 2, :], iota(P), row, None, ALU.is_equal)
                ts(onb[:, k % 2, 0:BLOCKS], iota(BLOCKS), blk, consts[:, C_GTOK + k:C_GTOK + k + 1], ALU.is_equal, ALU.mult)
                ts(onb[:, k % 2, BLOCKS:], iota(BLOCKS), blk, consts[:, C_STOK + k:C_STOK + k + 1], ALU.is_equal, ALU.mult
                   ).then_inc(S["list_ready"], 1)
            dve.wait_ge(S["list_done"], 2 * NT)
            ts(idx[:, :], duo[:, 0, 0:2 * BLOCKS], float(UNUSED), None, ALU.add).then_inc(S["idx_ready"], 1)

            def columns(e, par):
                dve.wait_ge(S["xth_done"], e + 1)
                tt(xt_lo[:, par, :, :].rearrange("p c t -> p (c t)"), pair[:, :, :].rearrange("p a b -> p (a b)"),
                   xt_hi[:, par, :, :].rearrange("p c t -> p (c t)").bitcast(F32), ALU.subtract).then_inc(S["xt_ready"], 1)

            columns(0, 0)
            with dve.Fori(0, EXPERTS // 2) as k:
                w = MOE(k)
                for par in range(2):
                    e = 2 * k + par
                    j0 = PER_EXPERT * par
                    for j in range(PER_EXPERT):
                        if j != 8:
                            tick(w, j0 + j)
                        if j == 6:
                            columns(e + 1, 1 - par)
                        if j == 8:
                            dve.wait_ge(S["unit_done"], w.u + j0 + 8)
                            dve.wait_ge(S["silu_done"], e + 2)
                            dve.wait_ge(S["bat_done"], e)
                            tt(ab[:, :], dense[0][:, 1, :], gs[:, :], ALU.mult).then_inc(S["u_free"], 1)
                            tick(w, j0 + j)
                        if j == 11:
                            dve.wait_ge(S["ath_done"], e + 1)
                            tt(at_lo[:, par, :, :].rearrange("p c t -> p (c t)"), duo[:, 0, :],
                               at_hi[:, par, :, :].rearrange("p c t -> p (c t)").bitcast(F32), ALU.subtract).then_inc(S["at_ready"], 1)
            for j in range(8):
                tick(Part(U_LAST), j)
            extra = dve.value_load(eint[0:1, EXTRA:EXTRA + 1])
            with dve.Fori(0, EXTRA) as b:
                with dve.If(extra > b):
                    dve.wait_ge(S["bg_ready"], b + 1)
                    tt(ab[:, :], dense[0][:, 1, :], gs[:, :], ALU.mult).then_inc(S["ba_ready"], 1)

            def back(t):
                dve.wait_ge(S["o2_done"], t + 1)
                tok = y1[:, :, t * P:(t + 1) * P]
                tt(tok, dense[t % 2][:, :, :].rearrange("p a (c t) -> p (a c) t", t=P), tok, ALU.add).then_inc(S["x2_ready"], 1)

            for t in range(NT):
                dve.wait_ge(y2_in[t % 2], 16 * (t // 2 + 1))
                need(dve, S["o2_done"], t - 1)
                step(ts(ot2[:, t % 2, :], y2b[:, t % 2, 0, :], wts[:, 0, t:t + 1], None, ALU.mult))
                stt(ot2[:, t % 2, :], y2b[:, t % 2, 1, :], wts[:, 1, t:t + 1], ot2[:, t % 2, :], ALU.mult, ALU.add
                    ).then_inc(S["o2_ready"], 1)
                if t:
                    back(t - 1)
            back(NT - 1)
            inverse(5, rrs[:, :])
            for c in range(KC):
                ins = scaled(res[:, c, META:], y1[:, c, :], col("norm_final_g", c), rrs[:, :])
            ins.then_inc(S["fr_done"], FROM["fr_done"])
            barrier(dve, 2)
            barrier(dve, 3)

            def two(ap):
                return ap.rearrange("p (h t) -> p h t", h=2)

            with dve.Fori(0, LAYERS) as l:
                dc.loop(l, 0, CHAIN)
                w = LAYER(l)
                n0 = 4 * KC + l * SQS
                x0 = 32 + l * FEED
                used = lambda d: 32 + l * USES + d // 2
                halves_of = lambda: pair[:, :, 0:HALF]

                def rms(k):
                    inverse(5 + l * 5 + k, rstd2[:, :])

                rms(1)
                dve.wait_ge(S["lpar_in"], l * 16 + 16)
                feed_normed(x0, val2, res, lambda c: lcol("mix_pre", c), rstd2[:, :], x_hi, x_lo, L)
                for j in range(5):
                    tick(w, j)
                    q = qb[:, j, :] if j < 4 else kb[:, :]
                    dve.wait_ge(S["rot_done"], l * 5 + j + 1)
                    need(dve, S["kv_ready"], l * 5 + j + 1)
                    dve.tensor_tensor(two(rot[:, :]), halves_of(), two(c2[:, D_SIN:D_SIN + L]), ALU.mult).then_inc(S["rot_used"], 1)
                    step(dve.tensor_tensor(q, q, c2[:, D_COS:D_COS + L], ALU.mult))
                    dve.wait_ge(S["rot_used"], l * 5 + j + 2)
                    dve.tensor_tensor(q, q, rot[:, :], ALU.add).then_inc(S["kv_ready"], 1)
                tick(w, 5)
                dve.wait_ge(S["pad_ready"], l + 1)
                for s in range(STEPS):
                    if s >= 5 and s % 2 == 1:
                        n = (s - 5) // 2
                        q0, nq = (0, META) if n == 0 else (META + P * (n - 1), P)
                        dve.wait_ge(S["os_ready"], l * QB + n + 1)
                        step(dve.reciprocal(orr[0:nq, 2:3], orr[0:nq, 1:2]))
                        o = ot[0:nq, n % 2, :, :].rearrange("p h d -> p (h d)")
                        dve.tensor_scalar(o, o, orr[0:nq, 2:3], None, ALU.mult).then_inc(S["o_ready"], 1)
                    if s < 10:
                        n, g, q0, nq, keys = item(s)
                        nk = sum(x[2] for x in keys)
                        dve.wait_ge(S["sc_done"], l * 10 + s + 1)
                        if s >= 2:
                            dve.wait_ge(S["pt_done"], l * PTS + ptseq(s - 2, 1) + 1)
                        mk = D_MASK[min(n, 2)]
                        x = sc[0:nq, s % 2, :, 0:nk]
                        M = lambda i: sm[0:nq, s % 4, i, :]
                        step(dve.scalar_tensor_tensor(x, duo[0:nq, :, :].rearrange("p a (b k) -> p (a b) k", b=2)[:, :, 0:nk], HD ** -0.5,
                                                      c2[0:nq, mk:mk + nk].unsqueeze(1).broadcast_to([nq, 4, nk]), ALU.mult, ALU.add))
                        step(dve.tensor_reduce(M(0), x, AX_X, ALU.max))
                        sinks = lcol("sinks", 4 * g, 4)[0:nq]
                        step(dve.tensor_tensor(M(0), M(0), sinks, ALU.max))
                        step(dve.tensor_scalar(M(1), M(0), -1.0, None, ALU.mult))
                        dve.tensor_tensor(M(2), sinks, M(0), ALU.subtract).then_inc(S["mk_ready"], 1)
                    if s >= 5 and s % 2 == 1:
                        dve.wait_ge(S["pt_done"], l * PTS + atseq(n_at := (s - 5) // 2) + 1)
                        q0, nq = (0, META) if n_at == 0 else (META + P * (n_at - 1), P)
                        dve.tensor_tensor(yat[:, :, q0:q0 + nq], pair[:, 1, :].rearrange("p (c t) -> p c t", c=4)[:, :, 0:nq],
                                          lcol("attn_g", 0, 4).unsqueeze(2).broadcast_to([P, 4, nq]), ALU.mult).then_inc(S["pt_free"], 1)
                    if s < 12:
                        tick(w, 6 + s)
                    if 0 <= s - 3 < 10:
                        i = s - 3
                        n, g, q0, nq, keys = item(i)
                        M = lambda k: sm[0:nq, i % 4, k, :]
                        dve.wait_ge(S["pv_done"], l * 10 + i + 2)
                        if n >= 2 and g == 0:
                            dve.wait_ge(S["pt_done"], l * PTS + atseq(n - 2) + 1)
                        step(dve.tensor_tensor(M(4), M(3), M(2), ALU.add))
                        step(dve.reciprocal(M(5), M(4)))
                        dve.tensor_tensor(ot[0:nq, n % 2, 4 * g:4 * g + 4, :], pair[0:nq, 0, 0:4 * HD].rearrange("p (h d) -> p h d", h=4),
                                          M(5).unsqueeze(2).broadcast_to([nq, 4, HD]), ALU.mult).then_inc(S["at2_ready"], 1)
                        if g == 1:
                            dve.wait_ge(S["at2_ready"], l * 10 + i + 2)
                            o = ot[0:nq, n % 2, :, :].rearrange("p h d -> p (h d)")
                            need(dve, S["om_ready"], l * QB + n + 1)
                            dve.scalar_tensor_tensor(rot[0:nq, 0:512], o, 1.0, o, ALU.mult, ALU.mult, accum_out=orr[0:nq, 0:1]
                                                     ).then_inc(S["om_ready"], 1)
                    if 8 <= s < 12:
                        m, j = s - 8, 6 + s
                        dve.wait_ge(S["unit_done"], w.u + j + 1)
                        dve.wait_ge(dense_free[(j - 4) % 2], used(j - 4) + 1)
                        dve.tensor_tensor(two(up[:, m, 2:]), dense[j % 2][:, :, 0:HALF], two(cb[:, m, :]), ALU.mult).then_inc(dense_free[j % 2], 1)
                        dve.wait_ge(dense_free[j % 2], used(j) + 1)
                        step(dve.tensor_scalar(cb[:, m, :], up[:, m, 0:L], lcol("conv_w", m * 3), None, ALU.mult))
                        for k in (1, 2):
                            step(dve.scalar_tensor_tensor(cb[:, m, :], up[:, m, k:k + L], lcol("conv_w", m * 3 + k), cb[:, m, :],
                                                          ALU.mult, ALU.add))
                        dve.tensor_tensor(cb[:, m, :], cb[:, m, :], bb[:, m, :], ALU.mult).then_inc(S["cv_ready"], 1)
                rms(2)
                for c in range(4):
                    scaled(cb[:, c, :], cb[:, c, :], lcol("conv_g", c), rstd2[:, :]).then_inc(S["val_ready"], 1)
                for c in range(8):
                    src = yat[:, c, :] if c < 4 else cb[:, c - 4, :]
                    low_part(x0 + 8 + c + 1, src, x_hi[:, c, :], x_lo[:, c, :])
                for m in range(8):
                    tick(w, L_OUT + m)

                def residual(n, gain, sem):
                    rms(n)
                    for c in range(KC):
                        step(scaled(fb[:, c, :], fb[:, c, :], lcol(gain, c), rstd2[:, :]))
                        dve.tensor_tensor(res[:, c, :], res[:, c, :], fb[:, c, :], ALU.add).then_inc(S[sem], 1)

                residual(3, "mix_post", "res_ready")
                dve.wait_ge(S["res_ready"], l * 8 + 8)
                rms(4)
                feed_normed(x0 + 16, val2, res, lambda c: lcol("mlp_pre", c), rstd2[:, :], x_hi, x_lo, L)
                with dve.Fori(0, QUARTERS) as q:
                    wq = LAYER(l, q)
                    xq = x0 + 24 + q * 8
                    for m in range(9):
                        if m:
                            j = L_MLP + m - 1
                            dve.wait_ge(dense_free[j % 2], 32 + l * USES + q * 8 + j // 2 + 1)
                            dve.wait_ge(S["x_ready"], xq + m - 3)
                            dve.tensor_tensor(val2[:, (m - 1) % 3, :], rl[:, (m - 1) % 2, :], rl[:, (m - 1) % 2, :], ALU.mult
                                              ).then_inc(S["val_ready"], 1)
                        tick(wq, L_MLP + m)
                        if m:
                            low_part(xq + m, val2[:, (m - 1) % 3, :], k_hi[:, m - 1, :], k_lo[:, m - 1, :])
                    for m in range(8):
                        if m:
                            tick(wq, L_MLP + 8 + m)
                        j = L_MLP + 8 + m
                        dve.wait_ge(S["unit_done"], wq.u + j + 1)
                        if m == 0:
                            dve.wait_ge(S["fb_zero"], l + 1)
                        dve.wait_ge(dense_free[j % 2], 32 + l * USES + q * 8 + j // 2 - 7)
                        dve.tensor_tensor(two(fb[:, m, :]), dense[j % 2][:, :, 0:HALF], two(fb[:, m, :]), ALU.add
                                          ).then_inc(dense_free[j % 2], 1)
                for j in range(L_DUMMY, PER_LAYER):
                    tick(w, j)
                residual(5, "mlp_post", "fr_done")
                dc.end(LAYERS)


def channels(v):
    return v.reshape(-1, P).T


def k_chunks(w):
    return w.reshape(-1, P, w.shape[-1])


def dense_units(w):
    n = w.shape[-1] // P
    return k_chunks(w).reshape(KC, P, n, P).transpose(2, 1, 0, 3).reshape(n, P, UNIT)


def half_units(w):
    return k_chunks(w).reshape(4, 2, P, 512).transpose(0, 2, 1, 3).reshape(4, P, UNIT)


def weight_stream(i):
    W = np.zeros((UNITS, P, UNIT), np.float32)
    w_in = i["w_in"][0]
    for u, c in ((U_A2, D), (U_A1, 0), (U_U, 2 * D), (U_GA, 4 * D), (U_GB, 5 * D)):
        W[u:u + 8] = dense_units(w_in[:, c:c + D])
    for h in range(2):
        W[U_V + 4 * h:U_V + 4 * h + 4] = half_units(w_in[:, 3 * D + h * 512:3 * D + (h + 1) * 512])
    for u, name in ((U_SGO, "w_sg_out"), (U_CVO, "w_conv_out"), (U_OUT, "w_out")):
        W[u:u + 8] = dense_units(i[name][0])
    for e in range(EXPERTS):
        u = U_MOE + e * PER_EXPERT
        W[u:u + 4] = half_units(i["w_expert_gate"][0, e])
        W[u + 4:u + 8] = half_units(i["w_expert_up"][0, e])
        d = u + PER_EXPERT + 8 if e < EXPERTS - 1 else U_LAST
        W[d:d + 4] = k_chunks(i["w_expert_down"][0, e])
    for l in range(LAYERS):
        u = U_LAYER + l * PER_LAYER
        w_in = i["w_in_2"][l]
        heads = w_in[:, 0:512].reshape(D, 2, 4, HD).transpose(0, 2, 1, 3).reshape(D, 512)
        W[u:u + 4] = dense_units(heads)
        W[u + 4:u + L_OUT] = dense_units(w_in[:, 512:])
        W[u + L_OUT:u + L_MLP] = dense_units(i["w_out_2"][l])
        for q in range(QUARTERS):
            m = u + L_MLP + 16 * q
            W[m:m + 8] = dense_units(i["w_up_2"][l][:, q * D:(q + 1) * D])
            W[m + 8:m + 16] = dense_units(i["w_down_2"][l][q * D:(q + 1) * D])
    return W


def everywhere(a):
    return np.broadcast_to(a, (P,) + a.shape)


def parameters(i):
    par = np.zeros((P, NPAR), np.float32)
    for name in COLS:
        v = i[name]
        if name == "conv_w":
            v = v[0].reshape(TAPS, KC, P).transpose(2, 1, 0).reshape(P, KC * TAPS)
        else:
            v = channels(v.reshape(-1))
        par[:, COLS[name]:COLS[name] + v.shape[1]] = v
    lpar = np.zeros((LAYERS, P, NLPAR), np.float32)
    for l in range(LAYERS):
        for name, v in (("mix_pre", channels(i["mix_pre_g_2"][l])), ("attn_g", channels(i["attn_out_g_2"][l])),
                        ("conv_g", channels(i["conv_out_g_2"][l])), ("mix_post", channels(i["mix_post_g_2"][l])),
                        ("mlp_pre", channels(i["mlp_pre_g_2"][l])), ("mlp_post", channels(i["mlp_post_g_2"][l])),
                        ("conv_w", i["conv_w_2"][l].reshape(3, AC, P).transpose(2, 1, 0).reshape(P, 12)),
                        ("sinks", everywhere(i["sinks_2"][l]))):
            lpar[l][:, LCOLS[name]:LCOLS[name] + v.shape[1]] = v
    return par, lpar


def constants():
    p = np.arange(P)
    cst = np.zeros((P, NCONST), np.float32)
    cst[:, C_IDENT:C_IDENT + P] = np.eye(P)
    cst[:, C_BEFORE:C_BEFORE + P] = p[:, None] < p[None, :]
    cst[:, C_ONE:C_ONE + P] = 1
    cst[:, C_MEAN:C_MEAN + P] = 1 / D
    cst[:, C_IOTA:C_IOTA + P] = p
    cst[:, C_EPS] = EPS
    for j in range(2):
        for t in range(NT):
            cst[:, C_GTOK + j * NT + t] = t * P + p - UNUSED
            cst[:, C_STOK + j * NT + t] = 2 * (t * P + p) + j - UNUSED
    c2 = np.zeros((P, NCONST2), np.float32)
    c2[:, D_MEAN:D_MEAN + P] = 1 / D
    c2[:, D_MEAN2:D_MEAN2 + P] = 2 / D
    c2[:, D_IDENT:D_IDENT + P] = np.eye(P)
    c2[:, D_EPS] = EPS
    rot = HD // 8
    freq = np.power(np.float32(500000.0), -np.arange(0, 2 * rot, 2, dtype=np.float32) / np.float32(2 * rot)).astype(np.float32)
    c2[:, D_COS:D_COS + L] = 1
    for h in range(0, P, HD):
        for d in range(rot):
            c2[h + rot + d, D_ROT + h + d] = -1
            c2[h + d, D_ROT + h + rot + d] = 1
            ang = (np.arange(L, dtype=np.float32) * freq[d]).astype(np.float32)
            for r in (h + d, h + rot + d):
                c2[r, D_COS:D_COS + L] = np.cos(ang)
                c2[r, D_SIN:D_SIN + L] = np.sin(ang)
    q = p[:, None]
    j = np.arange(META)[None]
    c2[:, D_MASK[0]:D_MASK[0] + META] = np.where(j <= q, 0, MASKED)
    j = np.arange(META + P)[None]
    c2[:, D_MASK[1]:D_MASK[1] + META + P] = np.where((j <= META + q) & (j > META + q - P), 0, MASKED)
    j = np.arange(2 * P)[None]
    c2[:, D_MASK[2]:D_MASK[2] + 2 * P] = np.where((j > q) & (j <= q + P), 0, MASKED)
    return cst, c2


def kernel(**inputs):
    import concourse.bacc as bacc
    from concourse.bass_utils import run_bass_kernel_spmd

    i = {k: np.asarray(v) for k, v in inputs.items()}
    par, lpar = parameters(i)
    cst, c2 = constants()
    router = np.concatenate([i["w_router_group"][0], i["w_router_expert"][0]], axis=1)
    arrays = {
        "W": weight_stream(i),
        "xT": i["x"][0].reshape(T, KC, P).transpose(2, 1, 0),
        "par": par, "lpar": lpar, "cst": cst, "cst2": c2,
        "bv": everywhere(i["b_in"][0, 3 * D:4 * D]),
        "bs": everywhere(i["b_sg"][0]),
        "wsT": i["w_sg"][0].transpose(2, 0, 1),
        "wr": k_chunks(router).transpose(1, 0, 2),
        "rb": everywhere(np.concatenate([i["b_router_group"][0], i["b_router_expert"][0]])),
        "metaT": i["meta_tokens_2"].reshape(META, KC, P).transpose(2, 1, 0),
    }
    nc = bacc.Bacc("TRN2", target_bir_lowering=False, num_devices=1)
    args, given = {}, {}
    for name, a in arrays.items():
        a = np.ascontiguousarray(a)
        given[f"in_{name}_dram"] = a
        args[name] = nc.dram_tensor(f"in_{name}_dram", a.shape, mybir.dt.from_np(a.dtype), kind="ExternalInput").ap()
    args["out"] = nc.dram_tensor("out_dram", (P, KC, T), F32, kind="ExternalOutput").ap()
    program(nc, **args)
    r = run_bass_kernel_spmd(nc, [given], core_ids=[0])
    got = r.results[0]["out_dram"]
    return np.ascontiguousarray(got.transpose(2, 1, 0).reshape(1, T, D))
```

```python
from contextlib import ExitStack

import numpy as np

import concourse.bass as bass
from concourse import mybir

ALU = mybir.AluOpType
ACT = mybir.ActivationFunctionType
F32 = mybir.dt.float32
F32R = mybir.dt.float32r
I32 = mybir.dt.int32
AX_X = mybir.AxisListType.X

P = 128
D = 1024
KC = D // P
T = 512
NT = T // P
TAPS = 31
PAD = TAPS - 1
HEADS_SG = 8
GROUPS, PER_GROUP = 4, 8
EXPERTS = GROUPS * PER_GROUP
ROUTER = GROUPS + EXPERTS
EXTRA = 2 * T // P - 1
BLOCKS = EXPERTS + EXTRA
UNUSED = 4096
EPS = 1e-6

LAYERS = 2
META = 16
L = T + META
HALF = L // 2
AC = 4
QB = 5
HD = 64
QUARTERS = 4
MASKED = -1.0e30

UNIT = 1024
RAW = 8
SPLIT = 4
AHEAD = SPLIT - 1
U_A2, U_A1, U_V, U_U, U_GA, U_GB, U_SGO, U_CVO, U_OUT = range(0, 72, 8)
U_MOE = 72
PER_EXPERT = 12
U_LAST = U_MOE + EXPERTS * PER_EXPERT
U_LAYER = U_LAST + 8
PER_LAYER = 96
U_END = U_LAYER + LAYERS * PER_LAYER
UNITS = U_END + 8
DVE_CONV = 6
TAPS_PER_STEP = 5
CHAIN = 85
L_OUT, L_MLP, L_DUMMY = 18, 26, 90

COLS = {}
_n = 0
for _name, _w in (("norm_mix_g", 8), ("b_in", 48), ("conv_w", 8 * TAPS), ("conv_b", 8), ("conv_ln_g", 8),
                  ("conv_ln_b", 8), ("b_conv_out", 8), ("sg_ln_g", 8), ("sg_ln_b", 8), ("b_sg_out", 8),
                  ("b_out", 8), ("norm_ffn_g", 8), ("norm_final_g", 8)):
    COLS[_name] = _n
    _n += _w
NPAR = _n
LCOLS = {}
_n = 0
for _name, _w in (("mix_pre", 8), ("attn_g", 4), ("conv_g", 4), ("mix_post", 8), ("mlp_pre", 8),
                  ("mlp_post", 8), ("conv_w", 12), ("sinks", 8)):
    LCOLS[_name] = _n
    _n += _w
NLPAR = _n

C_IDENT, C_BEFORE, C_ONE, C_MEAN, C_IOTA = 0, 128, 256, 384, 512
C_TOK = 640
C_GTOK = 648
C_STOK = 656
C_EPS = 664
NCONST = 665
D_MEAN, D_MEAN2, D_IDENT, D_ROT, D_COS, D_SIN = 0, 128, 256, 384, 512, 512 + L
D_MASK = (D_SIN + L, D_SIN + L + 16, D_SIN + L + 16 + 144)
D_EPS = D_MASK[2] + 256
NCONST2 = D_EPS + 1


FROM = {"silu_done": 1, "yb_ready": 1, "u_free": 1, "rot_used": 1, "kv_ready": 1,
        "pt_free": 1, "mk_ready": 1, "at2_ready": 1, "om_ready": 1, "pv_done": 1, "bat_done": 1, "fr_done": 9}


class Count:

    def __init__(self, eng, sem):
        self.eng, self.sem, self.base, self.n = eng, sem, 0, 0

    def add(self, ins):
        ins.then_inc(self.sem, 1)
        self.n += 1

    def wait(self, back=0):
        need(self.eng, self.sem, self.base + self.n - back)

    def loop(self, index, first, per):
        self.start, self.per = self.n, per
        self.base, self.first = self.base + (index - first) * per, first

    def end(self, times):
        assert self.n - self.start == self.per, (self.n - self.start, self.per)
        self.base, self.n = 0, self.start + times * self.per


def need(eng, sem, value):
    if not isinstance(value, int) or value > 0:
        eng.wait_ge(sem, value)


def program(nc, W, xT, par, lpar, cst, cst2, bv, bs, wsT, wr, rb, metaT, out):
    with ExitStack() as ctx:
        def sem(name):
            return ctx.enter_context(nc.semaphore(name))


        start = nc.sbuf_base + (-nc.sbuf_base) % 64
        size = (nc.sbuf_usable_end - start) // 64 * 64
        ctx.enter_context(nc.sbuf_tensor("arena", [P, size // 4], F32, align_bytes=64))
        where = {}

        class Map:

            def __init__(self, at):
                self.at = at

            def put(self, name, shape, dt=F32):
                n = 4
                for s in shape[1:]:
                    n *= s
                where[name] = self.at
                t = nc.alloc_sbuf_tensor_at(name, shape, dt, offset=self.at)
                self.at += (n + 63) // 64 * 64
                assert self.at <= start + size, (name, self.at - start - size)
                return t

        m = Map(start)
        raw = m.put("raw", [P, RAW, UNIT])
        w_hi = m.put("w_hi", [P, SPLIT, UNIT], F32R)
        w_lo = m.put("w_lo", [P, SPLIT, UNIT], F32R)
        x_hi = m.put("x_hi", [P, KC, L], F32R)
        x_lo = m.put("x_lo", [P, KC, L], F32R)
        low = m.at

        m = Map(low)
        pars = m.put("pars", [P, NPAR])
        consts = m.put("consts", [P, NCONST])
        y1 = m.put("y1", [P, KC, T])
        top = m.at
        stage = m.put("stage", [P, KC, T])
        apad = m.put("apad", [P, KC, T + PAD])
        ubuf = m.put("ubuf", [P, KC, T])
        gate_a = m.put("gate_a", [P, KC, T])
        bs_sb = m.put("bs_sb", [P, HEADS_SG, P])
        ws_sb = m.put("ws_sb", [P, HEADS_SG, P])
        val = m.put("val", [P, 3, T])
        sq = m.put("sq", [P, 2, T])
        rstd = m.put("rstd", [P, T])
        mu = m.put("mu", [P, T])
        vst = m.put("vst", [P, NT, 2, 6])
        vmv = m.put("vmv", [P, NT, 2])
        vrs = m.put("vrs", [P, NT])
        bv_sb = Map(where["gate_a"]).put("bv_sb", [P, D])
        xr = Map(where["apad"]).put("xr", [P, KC, T])
        vtok = stage[:, :, :].rearrange("p c t -> p (c t)").rearrange("p (n d) -> p n d", n=NT)

        m = Map(top)
        hb = m.put("hb", [P, KC, T])
        htok = m.put("htok", [P, NT, D])
        rrs = m.put("rrs", [P, T])
        wr_sb = m.put("wr_sb", [P, KC, ROUTER])
        rb_sb = m.put("rb_sb", [P, ROUTER])
        lg = m.put("lg", [P, NT, ROUTER])
        rt = m.put("rt", [P, 12, NT, EXPERTS])
        rs = m.put("rs", [P, 32, NT])
        onr = m.put("onr", [P, 2, P])
        onb = m.put("onb", [P, 2, 2 * BLOCKS])
        idx = m.put("idx", [P, 2 * BLOCKS], I32)
        eint = m.put("eint", [P, EXTRA + 1], I32)
        wts = m.put("wts", [P, 2, NT])
        gs = m.put("gs", [P, T])
        ab = m.put("ab", [P, T])
        xt_hi = m.put("xt_hi", [P, 2, KC, P], F32R)
        xt_lo = m.put("xt_lo", [P, 2, KC, P], F32R)
        at_hi = m.put("at_hi", [P, 2, 4, P], F32R)
        at_lo = m.put("at_lo", [P, 2, 4, P], F32R)
        yb = m.put("yb", [P, 2, D])
        lgT = m.put("lgT", [P, T])
        meta_sb = m.put("meta_sb", [P, KC, META])
        y2b = Map(where["hb"]).put("y2b", [P, 2, 2, D])
        m = Map(where["htok"])
        xg = m.put("xg", [P, 2, D])
        ot2 = m.put("ot2", [P, 2, D])
        tsq = Map(where["xt_lo"]).put("tsq", [P, 2, KC, P])
        bg = Map(where["x_hi"]).put("bg", [P, 4, UNIT])
        bu = Map(where["x_lo"]).put("bu", [P, 4, UNIT])
        bd = Map(where["hb"]).put("bd", [P, 4, UNIT])
        bx = Map(where["ot2"]).put("bx", [P, KC, P])
        ba = Map(where["at_hi"]).put("ba", [P, 4, P])

        m = Map(low)
        lp = m.put("lp", [P, NLPAR])
        k_hi = m.put("k_hi", [P, KC, L], F32R)
        k_lo = m.put("k_lo", [P, KC, L], F32R)
        res = m.put("res", [P, KC, L])
        fb = m.put("fb", [P, KC, L])
        kb = m.put("kb", [P, L])
        m.at = where["xt_hi"]
        c2 = m.put("c2", [P, NCONST2])
        vb = m.put("vb", [P, QB, P])
        sc = m.put("sc", [P, 2, 4, 256])
        pt = m.put("pt", [P, 2, 2, 4, P])
        ot = m.put("ot", [P, 2, 8, HD])
        val2 = m.put("val2", [P, 3, L])
        sq2 = m.put("sq2", [P, 2, L])
        rstd2 = Map(where["kb"]).put("rstd2", [P, L])
        sm = m.put("sm", [P, 4, 6, 4])
        orr = m.put("orr", [P, 4])
        m = Map(where["fb"])
        qb = m.put("qb", [P, AC, L])
        bb = m.put("bb", [P, AC, L])
        m = Map(where["k_hi"])
        cb = m.put("cb", [P, AC, L])
        up = m.put("up", [P, AC, L + 2])
        yat = m.put("yat", [P, AC, L])
        rot = m.put("rot", [P, L])
        m = Map(where["sc"])
        rl = m.put("rl", [P, 2, L])
        acc = m.put("acc", [P, L])
        assert where["res"] >= where["y1"] + 4 * KC * T

        dense = [ctx.enter_context(nc.psum_tensor(f"dense{i}", [P, 2, 512], F32)) for i in range(2)]
        pair = ctx.enter_context(nc.psum_tensor("pair", [P, 2, 512], F32))
        duo = ctx.enter_context(nc.psum_tensor("duo", [P, 2, 512], F32))
        hrows = nc.dram_tensor("hrows", [T, D], F32).ap()
        y2 = nc.dram_tensor("y2", [2 * T, D], F32).ap()

        names = """raw_in0 raw_in1 raw_in2 raw_in3 x_in0 x_in1 x_in2 x_in3 const_in par_in aux_in mask_in xr_in
            meta_in lpar_in out_done hi_done w_ready unit_done dense_free0 dense_free1 phase sq_ready
            sq_used val_ready xh_done x_ready dve_chain pool_chain v_sum v_gelu vn_ready rows_done
            sp_done sp_free conv_done s1_done pconv_done fb_zero yc_ready t_ready hb_ready lg_done
            lgt_ready tr_done ht_ready hrows_in ge_ready rank_ready rank_done list_ready list_done
            idx_ready xg_in0 xg_in1 xt_done xth_done xt_ready silu_done u_free ath_done at_ready yb_ready
            ys_out0 ys_out1 bx_in bw_in bx_done bx_ready bgu_done bs_done ba_ready bat_done bat_ready
            bd_done by_ready by_out y2_in0 y2_in1 o2_ready o2_done x2_ready res_ready rot_done rot_used
            kv_ready mk_ready ex_done sc_done pt_done pt_free pv_done o_ready at2_ready cv_ready fr_done
            total_done tsq_ready tsq_used inv_ready fs_ready root_ready ms_ready om_ready os_ready
            bg_ready gx_ready pad_ready""".split()
        S = {n: sem(n) for n in names}
        raw_in = [S[f"raw_in{i}"] for i in range(4)]
        dense_free = [S["dense_free0"], S["dense_free1"]]
        x_in = [S[f"x_in{i}"] for i in range(4)]
        xg_in = [S["xg_in0"], S["xg_in1"]]
        ys_out = [S["ys_out0"], S["ys_out1"]]
        y2_in = [S["y2_in0"], S["y2_in1"]]
        block = ctx.enter_context(nc.Block())

        def col(name, i):
            return pars[:, COLS[name] + i:COLS[name] + i + 1]

        def lcol(name, i, n=1):
            return lp[:, LCOLS[name] + i:LCOLS[name] + i + n]

        halves = ((0, HALF), (HALF, HALF))
        whole = ((0, T),)
        FEED = 56
        USES = 45
        SQS = 36
        VALS = 52
        STEPS = 14

        def item(i):
            n, g = i // 2, i % 2
            q0 = 0 if n == 0 else META + P * (n - 1)
            own = (n, q0, META if n == 0 else P)
            keys = [own] if n == 0 else [(n - 1, max(q0 - P, 0), META if n == 1 else P), own]
            return n, g, q0, own[2], keys

        pt_order = []
        for s in range(STEPS):
            if 0 <= s - 1 < 10:
                pt_order.append((s - 1, 0))
            if s >= 5 and s % 2 == 1:
                pt_order.append((s - 5) // 2)
            if 0 <= s - 1 < 10:
                pt_order.append((s - 1, 1))
        PTS = len(pt_order)
        ptseq = lambda i, hp: pt_order.index((i, hp))
        atseq = lambda n: pt_order.index(n)

        class Part:

            def __init__(self, u, u8=None):
                self.u, self.u8 = u, u // RAW if u8 is None else u8

        MOE = lambda k: Part(U_MOE + k * 24, U_MOE // RAW + k * 3)
        LAYER = lambda l, q=0: Part(U_LAYER + l * PER_LAYER + q * 16, U_LAYER // RAW + l * (PER_LAYER // RAW) + q * 2)


        @block.sync
        def _(sp):
            sp.dma_start(consts[:, :], cst).then_inc(S["const_in"], 16)
            for i in range(4):
                sp.dma_start(stage[:, 2 * i:2 * i + 2, :], xT[:, 2 * i:2 * i + 2, :]).then_inc(x_in[i], 16)
            sp.dma_start(pars[:, :], par).then_inc(S["par_in"], 16)
            for i in range(4):
                sp.dma_start(raw[:, 2 * i:2 * i + 2, :],
                             W[2 * i:2 * i + 2].rearrange("u p n -> p u n")).then_inc(raw_in[i], 16)
            with sp.Fori(1, UNITS // RAW) as r:
                for i in range(4):
                    sp.wait_ge(S["w_ready"], (r - 1) * RAW + 2 * i + 2)
                    sp.dma_start(raw[:, 2 * i:2 * i + 2, :],
                                 W[bass.ds(r * RAW + 2 * i, 2)].rearrange("u p n -> p u n")).then_inc(raw_in[i], 16)
            sp.wait_ge(S["fr_done"], 8 * LAYERS + 9)
            sp.dma_start(out, res[:, :, META:]).then_inc(S["out_done"], 16)
            sp.wait_ge(S["out_done"], 16)

        def barrier(eng, n):
            eng.drain().then_inc(S["phase"], 1)
            eng.wait_ge(S["phase"], 4 * n)

        @block.gpsimd
        def _(pool):
            pc = Count(pool, S["pool_chain"])
            for i in range(4):
                pool.wait_ge(raw_in[i], 16)
            pool.dma_start(bv_sb[:, :], bv).then_inc(S["aux_in"], 16)
            pool.dma_start(bs_sb[:, :, :], bs).then_inc(S["aux_in"], 16)
            pool.dma_start(ws_sb[:, :, :], wsT).then_inc(S["aux_in"], 16)
            pc.add(pool.memset(apad[:, :, 0:PAD], 0.0))
            pool.wait_ge(S["aux_in"], 48)
            pc.wait()
            pc.add(pool.memset(ws_sb[64:128, :, 0:64], 0.0))
            pc.wait()
            pool.wait_ge(S["sq_used"], KC)
            own = range(DVE_CONV, KC)
            for k in range(TAPS):
                for c in own:
                    wc = col("conv_w", c * TAPS + k)
                    src = apad[:, c, k:k + T]
                    if k == 0:
                        pool.wait_ge(dense_free[c % 2], (U_A1 + c) // 2 + 1)
                        pc.add(pool.tensor_scalar(y1[:, c, :], src, wc, col("conv_b", c), ALU.mult, ALU.add))
                    else:
                        pc.add(pool.tensor_scalar(sq[:, c % 2, :], src, wc, None, ALU.mult))
                if k:
                    for c in own:
                        pc.wait(len(own) - 1)
                        pc.add(pool.tensor_tensor(y1[:, c, :], y1[:, c, :], sq[:, c % 2, :], ALU.add))
                pc.wait()
            pool.drain().then_inc(S["pconv_done"], 1)
            pool.wait_ge(S["conv_done"], DVE_CONV * TAPS)
            pool.dma_start(xr[:, :, :], xT).then_inc(S["xr_in"], 16)
            pool.wait_ge(S["xr_in"], 16)
            barrier(pool, 1)

            pool.dma_start(wr_sb[:, :, :], wr).then_inc(S["mask_in"], 16)
            pool.dma_start(rb_sb[:, :], rb).then_inc(S["mask_in"], 16)
            pool.dma_start(meta_sb[:, :, :], metaT).then_inc(S["meta_in"], 16)
            pool.wait_ge(S["hrows_in"], 16 * NT)
            pc.add(pool.memset(xg[:, :, :], 0.0))
            pc.wait()

            def gather(e):
                if e >= 2:
                    pool.wait_ge(S["xt_done"], e - 1)
                if e == 0:
                    pool.wait_ge(S["idx_ready"], 1)
                pool.indirect_dma_start(
                    out=xg[:, e % 2, :], out_offset=None, in_=hrows,
                    in_offset=bass.IndirectOffsetOnAxis(ap=idx[:, e:e + 1], axis=0),
                    bounds_check=T - 1, oob_is_err=False).then_inc(xg_in[e % 2], 16)

            def scatter(e, src, done):
                pool.indirect_dma_start(
                    out=y2, out_offset=bass.IndirectOffsetOnAxis(ap=idx[:, BLOCKS + e:BLOCKS + e + 1], axis=0),
                    in_=src, in_offset=None,
                    bounds_check=2 * T - 1, oob_is_err=False).then_inc(done, 16)

            gather(0)
            gather(1)
            gather(2)
            for s in range(1, EXPERTS + 1):
                if s + 2 <= EXPERTS:
                    gather(s + 2)
                if s == EXPERTS:
                    pool.wait_ge(S["unit_done"], U_LAST - 4)
                    pool.wait_ge(S["xt_ready"], EXPERTS + 1)
                    pool.dma_start(c2[:, :], cst2).then_inc(S["meta_in"], 16)
                pool.wait_ge(S["yb_ready"], s + 2)
                scatter(s - 1, yb[:, s % 2, :], ys_out[s % 2])
            pool.wait_ge(ys_out[1], 16 * EXPERTS // 2)
            pool.wait_ge(ys_out[0], 16 * EXPERTS // 2)
            pool.wait_ge(S["xt_done"], EXPERTS + 1)
            extra = pool.value_load(eint[0:1, EXTRA:EXTRA + 1])
            for b in range(EXTRA):
                with pool.If(extra > b):
                    pool.indirect_dma_start(
                        out=xg[:, 0, :], out_offset=None, in_=hrows,
                        in_offset=bass.IndirectOffsetOnAxis(ap=idx[:, EXPERTS + b:EXPERTS + b + 1], axis=0),
                        bounds_check=T - 1, oob_is_err=False).then_inc(S["bx_in"], 16)
                    pool.wait_ge(S["by_ready"], b + 1)
                    scatter(EXPERTS + b, yb[:, 0, :], S["by_out"])
                    pool.wait_ge(S["by_out"], 16 * (b + 1))
            for t in range(NT):
                if t >= 2:
                    pool.wait_ge(S["o2_ready"], t - 1)
                pool.dma_start(y2b[:, t % 2, :, :],
                               y2[2 * t * P:2 * (t + 1) * P, :].rearrange("(p j) d -> p j d", j=2)
                               ).then_inc(y2_in[t % 2], 16)
            pool.wait_ge(S["meta_in"], 32)
            barrier(pool, 2)
            with pool.Fori(0, LAYERS) as l:
                need(pool, S["fr_done"], l * 8 + 9)
                pool.dma_start(lp[:, :], lpar[l]).then_inc(S["lpar_in"], 16)
                pool.memset(up[:, :, 0:2], 0.0).then_inc(S["pad_ready"], 1)

                def by_root(k):
                    pool.wait_ge(S["inv_ready"], l * 2 + k)
                    for c in range(KC):
                        pool.tensor_tensor(fb[:, c, :], fb[:, c, :], rstd2[:, :], ALU.mult).then_inc(S["fs_ready"], 1)
                        pool.wait_ge(S["fs_ready"], l * 16 + (k - 1) * 8 + c + 1)

                by_root(1)
                mixed = pool.to_reg(l * 8 + 8)
                pool.wait_ge(S["meta_in"], 32)
                pool.wait_ge(S["res_ready"], mixed)
                pool.memset(fb[:, :, :], 0.0).then_inc(S["fb_zero"], 1)
                by_root(2)
        @block.tensor
        def _(pe):
            def dense_unit(w, j, use, which, parts, hi, lo, fed=None, order=range(KC), beside=None):
                need(pe, S["w_ready"], w.u + j + 1)
                need(pe, dense_free[which], use)
                s = j % SPLIT
                for i, kc in enumerate(order):
                    if fed is not None:
                        need(pe, S["x_ready"], fed + i + 1)
                    c = slice(kc * P, (kc + 1) * P)
                    for wt, x in ((w_hi, hi), (w_hi, lo), (w_lo, hi)):
                        for h, (t0, n) in enumerate(parts):
                            last = pe.matmul(dense[which][:, h, 0:n], wt[:, s, c], x[:, kc, t0:t0 + n],
                                             start=(i == 0 and wt is w_hi and x is hi),
                                             stop=(i == KC - 1 and wt is w_lo))
                    if beside is not None and i < KC - 1:
                        beside(kc)
                last.then_inc(S["unit_done"], 1)
                if beside is not None:
                    beside(KC - 1)

            def sums(chunks, n0, ones, src, parts, ready="sq_ready", used="sq_used", only=None, bank=pair):
                for c in range(chunks) if only is None else only:
                    need(pe, S[ready], n0 + c + 1)
                    for h, (t0, n) in enumerate(parts):
                        last = pe.matmul(bank[:, h, 0:n], ones, src(c)[:, t0:t0 + n], start=(c == 0), stop=(c == chunks - 1))
                    last.then_inc(S[used], 1)

            for name in ("pv_done", "bat_done"):
                pe.drain().then_inc(S[name], FROM[name])
            def total(n, ones, src, parts):
                pe.wait_ge(S["sq_used"], n)
                for h, (t0, w) in enumerate(parts):
                    last = pe.matmul(pair[:, h, 0:w], ones, src[:, t0:t0 + w], start=True, stop=True)
                last.then_inc(S["total_done"], 1)

            mean = consts[:, C_MEAN:C_MEAN + P]
            ident = consts[:, C_IDENT:C_IDENT + P]
            pe.wait_ge(S["const_in"], 16)
            sums(KC, 0, mean, lambda c: sq[:, c % 2, :], whole)

            def run(u0, fed=None):
                for m in range(8):
                    d = (u0 if u0 < U_V else u0 - 8) + m
                    dense_unit(Part(u0), m, d // 2, d % 2, whole, x_hi, x_lo, fed if m == 0 else None)

            run(U_A2, fed=0)
            run(U_A1)
            for h in range(2):
                for i in range(2):
                    need(pe, dense_free[i], 8)
                for j in range(4):
                    u = U_V + 4 * h + j
                    need(pe, S["w_ready"], u + 1)
                    for kk in range(2):
                        kc = 2 * j + kk
                        for t in range(NT):
                            bank = (dense[0], dense[1], pair, duo)[2 * h + t // 2][:, t % 2, :]
                            for x, wt in ((x_hi, w_hi), (x_hi, w_lo), (x_lo, w_hi)):
                                last = pe.matmul(bank, x[:, kc, t * P:(t + 1) * P], wt[:, u % SPLIT, kk * 512:(kk + 1) * 512],
                                                 start=(kc == 0 and x is x_hi and wt is w_hi), stop=(kc == KC - 1 and x is x_lo))
                    last.then_inc(S["unit_done"], 1)
            pe.wait_ge(S["v_sum"], 4)
            run(U_U)
            pe.wait_ge(S["v_sum"], 8)
            pe.wait_ge(S["pool_chain"], 2)
            for h in range(2):
                last = pe.matmul(pair[:, h, :], consts[:, C_ONE:C_ONE + P],
                                 ws_sb[:, 4 * h:4 * h + 4, :].rearrange("p h q -> p (h q)"), start=True, stop=True)
            last.then_inc(S["rows_done"], 1)
            pe.wait_ge(S["vn_ready"], NT)
            for m in range(8):
                d = U_GA - 8 + m
                dense_unit(Part(U_GA), m, d // 2, d % 2, whole, x_hi, x_lo)
                need(pe, S["sp_free"], m - 1)
                for n in range(NT):
                    last = pe.matmul(duo[:, m % 2, n * P:(n + 1) * P], vtok[:, n, m * P:(m + 1) * P], ws_sb[:, m, :],
                                     start=True, stop=True)
                last.then_inc(S["sp_done"], 1)
            run(U_GB)
            pe.wait_ge(S["sp_free"], 8)
            for m in range(8):
                d = U_SGO - 8 + m
                dense_unit(Part(U_SGO), m, d // 2, d % 2, whole, x_hi, x_lo, 8 if m == 0 else None)
                if m == 1:
                    pe.wait_ge(S["conv_done"], DVE_CONV * TAPS)
                    pe.wait_ge(S["pconv_done"], 1)
                    sums(KC, -KC, mean, lambda c: y1[:, c, :], whole, used="s1_done")
                if m == 3:
                    sums(KC, KC, mean, lambda c: sq[:, c % 2, :], whole)
            run(U_CVO, fed=16)
            for m in range(8):
                d = U_OUT - 8 + m
                dense_unit(Part(U_OUT), m, d // 2, d % 2, whole, x_hi, x_lo, 24 if m == 0 else None)
            total(3 * KC, mean, mu, whole)
            barrier(pe, 1)

            pe.wait_ge(S["mask_in"], 32)
            for kc in range(KC):
                pe.wait_ge(S["hb_ready"], kc + 1)
                last = pe.matmul(duo[0:ROUTER, 0, :], wr_sb[:, kc, :], hb[:, kc, :], start=(kc == 0), stop=(kc == KC - 1))
            last.then_inc(S["lg_done"], 1)
            pe.wait_ge(S["lgt_ready"], 1)
            for t in range(NT):
                last = pe.transpose(duo[:, 1, t * ROUTER:(t + 1) * ROUTER], lgT[0:ROUTER, t * P:(t + 1) * P],
                                    consts[0:ROUTER, C_IDENT:C_IDENT + ROUTER])
            last.then_inc(S["lg_done"], 1)
            for t in range(NT):
                need(pe, S["ht_ready"], t - 1)
                for c in range(KC):
                    last = pe.transpose(dense[t % 2][:, c // 4, (c % 4) * P:(c % 4 + 1) * P], hb[:, c, t * P:(t + 1) * P], ident)
                last.then_inc(S["tr_done"], 1)
            pe.wait_ge(S["rank_ready"], 1)
            msum = rt[:, 6, :, :]
            for t in range(NT + 1):
                for s in range(min(t + 1, NT)):
                    lhs = C_BEFORE if s == t else C_ONE
                    last = pe.matmul(duo[:, 1, t * EXPERTS:(t + 1) * EXPERTS], consts[:, lhs:lhs + P], msum[:, s, :],
                                     start=(s == 0), stop=(s == min(t, NT - 1)))
            last.then_inc(S["rank_done"], 1)
            for k in range(2 * NT):
                pe.wait_ge(S["list_ready"], k + 1)
                pe.matmul(duo[:, 0, 0:2 * BLOCKS], onr[:, k % 2, :], onb[:, k % 2, :],
                          start=(k == 0), stop=(k == 2 * NT - 1)).then_inc(S["list_done"], 1)

            def rows_to_columns(e, par):
                need(pe, xg_in[par], 16 * (e // 2 + 1) if isinstance(e, int) else 16 * e)
                for c in range(KC):
                    last = pe.transpose(pair[:, c // 4, (c % 4) * P:(c % 4 + 1) * P], xg[:, par, c * P:(c + 1) * P], ident)
                last.then_inc(S["xt_done"], 1)

            rows_to_columns(0, 0)

            def expert(k, w, par):
                e = 2 * k + par
                j0 = PER_EXPERT * par
                pe.wait_ge(S["xt_ready"], e + 1)
                for j in range(8):
                    if j == 0:
                        need(pe, S["silu_done"], e + 1)
                    if j == 4:
                        need(pe, xg_in[1 - par], 16 * (k + 1 + par))
                        for c in range(KC):
                            last = pe.transpose(pair[:, c // 4, (c % 4) * P:(c % 4 + 1) * P],
                                                xg[:, 1 - par, c * P:(c + 1) * P], ident)
                        last.then_inc(S["xt_done"], 1)
                        need(pe, S["u_free"], e + 1)
                    s = (j0 + j) % SPLIT
                    pe.wait_ge(S["w_ready"], w.u + j0 + j + 1)
                    for kk in range(2):
                        kc = (2 * j + kk) % KC
                        for x, wt in ((xt_hi, w_hi), (xt_hi, w_lo), (xt_lo, w_hi)):
                            last = pe.matmul(dense[0][:, j // 4, :], x[:, par, kc, :], wt[:, s, kk * 512:(kk + 1) * 512],
                                             start=(kc == 0 and x is xt_hi and wt is w_hi), stop=(kc == KC - 1 and x is xt_lo))
                    last.then_inc(S["unit_done"], 1)
                need(pe, S["yb_ready"], e + 1)
                for j in range(4):
                    down(w, j0 + 8 + j, j, 1 - par, e)
                    if j == 2:
                        pe.wait_ge(S["u_free"], e + 2)
                        need(pe, S["at_ready"], e + 1)
                        for c in range(4):
                            last = pe.transpose(duo[:, 0, c * P:(c + 1) * P], ab[:, c * P:(c + 1) * P], ident)
                        last.then_inc(S["bat_done"], 1)

            def down(w, ju, j, par, e):
                pe.wait_ge(S["w_ready"], w.u + ju + 1)
                if j == 0:
                    pe.wait_ge(S["at_ready"], e + 1)
                for x, wt in ((at_hi, w_hi), (at_hi, w_lo), (at_lo, w_hi)):
                    for h in range(2):
                        last = pe.matmul(dense[1][:, h, :], x[:, par, j, :], wt[:, ju % SPLIT, h * 512:(h + 1) * 512],
                                         start=(j == 0 and x is at_hi and wt is w_hi), stop=(j == 3 and x is at_lo))
                last.then_inc(S["unit_done"], 1)

            pe.wait_ge(S["idx_ready"], 1)
            with pe.Fori(0, EXPERTS // 2) as k:
                for par in range(2):
                    expert(k, MOE(k), par)
            pe.wait_ge(S["yb_ready"], EXPERTS + 1)
            for j in range(4):
                down(Part(U_LAST), j, j, 1, EXPERTS)
            pe.drain().then_inc(S["unit_done"], 4)
            pe.wait_ge(S["yb_ready"], EXPERTS + 2)
            pe.wait_ge(S["xt_ready"], EXPERTS + 1)
            extra = pe.value_load(eint[0:1, EXTRA:EXTRA + 1])
            with pe.Fori(0, EXTRA) as b:
                with pe.If(extra > b):
                    pe.wait_ge(S["bx_in"], b * 16 + 16)
                    for c in range(KC):
                        last = pe.transpose(pair[:, c // 4, (c % 4) * P:(c % 4 + 1) * P], xg[:, 0, c * P:(c + 1) * P], ident)
                    last.then_inc(S["bx_done"], 1)
                    pe.wait_ge(S["bx_ready"], b + 1)
                    pe.wait_ge(S["bw_in"], b * 48 + 48)
                    for h, wt in enumerate((bg, bu)):
                        for kc in range(KC):
                            last = pe.matmul(dense[0][:, h, :], bx[:, kc, :], wt[:, kc // 2, (kc % 2) * 512:(kc % 2 + 1) * 512],
                                             start=(kc == 0), stop=(kc == KC - 1))
                    last.then_inc(S["bgu_done"], 1)
                    pe.wait_ge(S["ba_ready"], b + 1)
                    for c in range(4):
                        last = pe.transpose(duo[:, 0, c * P:(c + 1) * P], ab[:, c * P:(c + 1) * P], ident)
                    last.then_inc(S["bs_done"], 1)
                    pe.wait_ge(S["bat_ready"], b + 1)
                    for h in range(2):
                        for c in range(4):
                            last = pe.matmul(dense[1][:, h, :], ba[:, c, :], bd[:, c, h * 512:(h + 1) * 512],
                                             start=(c == 0), stop=(c == 3))
                    last.then_inc(S["bd_done"], 1)
            def tile_sum(t):
                pe.wait_ge(S["tsq_ready"], t + 1)
                for c in range(KC):
                    last = pe.matmul(pair[:, 0, t * P:(t + 1) * P], mean, tsq[:, t % 2, c, :], start=(c == 0), stop=(c == KC - 1))
                last.then_inc(S["tsq_used"], 1)

            for t in range(NT):
                pe.wait_ge(S["o2_ready"], t + 1)
                need(pe, S["x2_ready"], t - 1)
                for c in range(KC):
                    last = pe.transpose(dense[t % 2][:, c // 4, (c % 4) * P:(c % 4 + 1) * P], ot2[:, t % 2, c * P:(c + 1) * P], ident)
                last.then_inc(S["o2_done"], 1)
                if t:
                    tile_sum(t - 1)
            tile_sum(NT - 1)
            barrier(pe, 2)

            cmean = c2[:, D_MEAN:D_MEAN + P]
            rotm = c2[:, D_ROT:D_ROT + P]
            sqs = lambda c: sq2[:, c % 2, :]
            with pe.Fori(0, LAYERS) as l:
                w = LAYER(l)
                n0 = 3 * KC + l * SQS
                fed0 = 32 + l * FEED
                use = lambda d: 32 + l * USES + d // 2
                sums(KC, n0, cmean, sqs, halves)

                def rotate(j):
                    need(pe, dense_free[j % 2], use(j) + 1)
                    need(pe, S["rot_used"], l * 5 + j + 1)
                    src = qb[:, j, :] if j < 4 else kb[:, :]
                    for h, (t0, n) in enumerate(halves):
                        last = pe.matmul(pair[:, h, 0:n], rotm, src[:, t0:t0 + n], start=True, stop=True)
                    last.then_inc(S["rot_done"], 1)

                for j in range(5):
                    dense_unit(w, j, use(j), j % 2, halves, x_hi, x_lo, fed0 if j == 0 else None)
                    if j:
                        rotate(j - 1)
                need(pe, S["w_ready"], w.u + 6)
                need(pe, dense_free[1], use(5))
                for t in range(QB):
                    t0, n = (0, META) if t == 0 else (META + P * (t - 1), P)
                    for kc in range(KC):
                        for x, wt in ((x_hi, w_hi), (x_hi, w_lo), (x_lo, w_hi)):
                            last = pe.matmul(dense[1][0:n, t // 4, (t % 4) * P:(t % 4 + 1) * P], x[:, kc, t0:t0 + n],
                                             wt[:, 5 % SPLIT, kc * P:(kc + 1) * P],
                                             start=(kc == 0 and x is x_hi and wt is w_hi), stop=(kc == KC - 1 and x is x_lo))
                last.then_inc(S["unit_done"], 1)
                rotate(4)

                def narrow_need(n, sem, value):
                    if n == 0:
                        value = pe.to_reg(value)
                        pe.wait_ge(S["const_in"], 16)
                    need(pe, sem, value)

                def transposes(i, hp):
                    n, g, q0, nq, keys = item(i)
                    if hp == 0:
                        pe.wait_ge(S["ex_done"], l * 10 + i + 1)
                    narrow_need(n, S["pt_free"], l * PTS + ptseq(i, hp) + 1)
                    k0 = 0
                    for kt, (_, _, nk) in enumerate(keys):
                        for h in range(2):
                            o = (2 * kt + h) * P
                            last = pe.transpose(pair[0:nk, 1, o:o + nq], sc[0:nq, i % 2, 2 * hp + h, k0:k0 + nk], c2[0:nq, D_IDENT:D_IDENT + nq])
                        k0 += nk
                    last.then_inc(S["pt_done"], 1)

                dense_unit(w, 6, use(6), 0, halves, x_hi, x_lo)
                need(pe, dense_free[1], use(5) + 1)
                pe.wait_ge(S["kv_ready"], l * 5 + 6)
                for s in range(STEPS):
                    if 10 <= s < 13:
                        pe.wait_ge(S["mk_ready"], l * 10 + 11)
                        sums(4, n0 + 8, c2[:, D_MEAN2:D_MEAN2 + P], sqs, halves, only=[s - 10], bank=duo)
                    if s < 10:
                        n, g, q0, nq, keys = item(s)
                        narrow_need(n, S["mk_ready"], l * 10 + s + 1)
                        k0, nk = keys[0][1], sum(x[2] for x in keys)
                        for h in range(4):
                            r = slice(g * HD, (g + 1) * HD)
                            last = pe.matmul(duo[0:nq, h // 2, (h % 2) * 256:(h % 2) * 256 + nk], qb[r, h, q0:q0 + nq],
                                             kb[r, k0:k0 + nk], start=True, stop=True)
                        last.then_inc(S["sc_done"], 1)
                    if 0 <= s - 1 < 10:
                        transposes(s - 1, 0)
                    if 0 < s < 12:
                        dense_unit(w, 6 + s, use(6 + s), s % 2, halves, x_hi, x_lo)
                    if s >= 5 and s % 2 == 1:
                        n = (s - 5) // 2
                        nq = META if n == 0 else P
                        pe.wait_ge(S["o_ready"], l * QB + n + 1)
                        narrow_need(n, S["pt_free"], l * PTS + atseq(n) + 1)
                        for c in range(4):
                            last = pe.transpose(pair[:, 1, c * P:c * P + nq],
                                                ot[0:nq, n % 2, 2 * c:2 * c + 2, :].rearrange("p h d -> p (h d)"), c2[0:nq, D_IDENT:D_IDENT + nq])
                        last.then_inc(S["pt_done"], 1)
                    if 0 <= s - 1 < 10:
                        transposes(s - 1, 1)
                    if 0 <= s - 2 < 10:
                        i = s - 2
                        n, g, q0, nq, keys = item(i)
                        narrow_need(n, S["at2_ready"], l * 10 + i + 1)
                        narrow_need(n, S["pt_free"], l * PTS + ptseq(i, 1) + 2)
                        for h in range(4):
                            for kt, (tile, _, nk) in enumerate(keys):
                                last = pe.matmul(pair[0:nq, 0, h * HD:(h + 1) * HD], pt[0:nk, i % 2, kt, h, 0:nq],
                                                 vb[0:nk, tile, g * HD:(g + 1) * HD], start=(kt == 0), stop=(kt == len(keys) - 1))
                        last.then_inc(S["pv_done"], 1)
                    if s == 12:
                        sums(4, n0 + 8, c2[:, D_MEAN2:D_MEAN2 + P], sqs, halves, only=[3], bank=duo)
                for j in range(L_OUT, L_MLP):
                    dense_unit(w, j, use(j), j % 2, halves, x_hi, x_lo, fed0 + 8 if j == L_OUT else None, (4, 5, 6, 7, 0, 1, 2, 3))
                total(n0 + 20, cmean, acc, halves)

                def quarter(q, beside=None):
                    wq = LAYER(l, q)
                    useq = lambda d: 32 + l * USES + q * 8 + d // 2
                    for m in range(8):
                        j = L_MLP + m
                        dense_unit(wq, j, useq(j), j % 2, halves, x_hi, x_lo, fed0 + 16 if m == 0 else None,
                                   beside=beside if m == 0 else None)
                    for m in range(8):
                        j = L_MLP + 8 + m
                        dense_unit(wq, j, useq(j), j % 2, halves, k_hi, k_lo, fed0 + 24 + q * 8 if m == 0 else None)

                quarter(0, lambda kc: sums(KC, n0 + 20, cmean, sqs, halves, only=[kc]))
                with pe.Fori(1, QUARTERS) as q:
                    quarter(q)
                pe.wait_ge(S["w_ready"], w.u + L_DUMMY + AHEAD)
                pe.drain().then_inc(S["unit_done"], PER_LAYER - L_DUMMY)
                total(n0 + 36, cmean, acc, halves)

        @block.scalar
        def _(act):
            for name in ("silu_done", "yb_ready"):
                act.drain().then_inc(S[name], FROM[name])

            def tick(w, j):
                v = j + AHEAD
                act.wait_ge(raw_in[v % RAW // 2], (w.u8 + v // RAW) * 16 + 16)
                need(act, S["unit_done"], w.u + v - SPLIT + 1)
                act.activation(w_hi[:, v % SPLIT, :], raw[:, v % RAW, :], ACT.Copy).then_inc(S["hi_done"], 1)

            def skip(w, j, n):
                for v in range(j + AHEAD, j + AHEAD + n):
                    act.wait_ge(raw_in[v % RAW // 2], (w.u8 + v // RAW) * 16 + 16)
                act.drain().then_inc(S["hi_done"], n)

            def high(src, dst, ready=None):
                if ready is not None:
                    act.wait_ge(S["val_ready"], ready)
                act.activation(dst, src, ACT.Copy).then_inc(S["xh_done"], 1)

            def square(n, dst, src):
                need(act, S["sq_used"], n - 1)
                act.activation(dst, src, ACT.Square).then_inc(S["sq_ready"], 1)

            def root(n, out, src):
                act.wait_ge(S["sq_used"], n)
                act.activation(out, src, ACT.Sqrt, bias=consts[:, C_EPS:C_EPS + 1]).then_inc(S["root_ready"], 1)

            def total_root(k, n, out, src):
                act.wait_ge(S["total_done"], k)
                act.wait_ge(S["sq_used"], n)
                act.activation(out, src, ACT.Sqrt, bias=consts[:, C_EPS:C_EPS + 1]).then_inc(S["root_ready"], 1)

            def evac(u, which, out, func, bias=0.0):
                act.wait_ge(S["unit_done"], u + 1)
                return act.activation(out, dense[which][:, 0, :], func, bias=bias)

            for c in range(KC):
                act.wait_ge(x_in[c // 2], 16)
                square(c, sq[:, c % 2, :], stage[:, c, :])
            for j in range(-AHEAD, 0):
                tick(Part(0), j)
            act.wait_ge(S["const_in"], 16)
            act.wait_ge(S["par_in"], 16)
            root(KC, rstd[:, :], pair[:, 0, :])
            for c in range(KC):
                high(val[:, c % 3, :], x_hi[:, c, 0:T], c + 1)
            for m in range(8):
                tick(Part(U_A2), m)
                d = m
                evac(U_A2 + m, d % 2, stage[:, m, :], ACT.Sigmoid, col("b_in", 8 + m)).then_inc(dense_free[d % 2], 1)
            for m in range(8):
                tick(Part(U_A1), m)
            for j in range(8):
                tick(Part(U_V), j)
                if j % 4 == 3:
                    for t in range(NT):
                        k = NT * (j // 4) + t
                        act.wait_ge(S["v_sum"], k + 1)
                        v = vtok[:, t, (j // 4) * 512:(j // 4 + 1) * 512]
                        act.activation(v, v, ACT.Gelu).then_inc(S["v_gelu"], 1)
            for m in range(8):
                tick(Part(U_U), m)
                if m == 0:
                    act.wait_ge(S["ms_ready"], 1)
                    act.activation(vrs[:, :], vmv[:, :, 1], ACT.Sqrt, bias=consts[:, C_EPS:C_EPS + 1]).then_inc(S["root_ready"], 1)
                d = U_U - 8 + m
                ins = evac(U_U + m, d % 2, ubuf[:, m, :], ACT.Gelu, col("b_in", 16 + m))
                ins.then_inc(dense_free[d % 2], 1)
            for m in range(8):
                tick(Part(U_GA), m)
                d = U_GA - 8 + m
                if m == 0:
                    act.wait_ge(S["v_sum"], 8)
                evac(U_GA + m, d % 2, gate_a[:, m, :], ACT.Sigmoid, col("b_in", 32 + m)).then_inc(dense_free[d % 2], 1)
            for m in range(8):
                tick(Part(U_GB), m)
                d = U_GB - 8 + m
                if m == 0:
                    act.wait_ge(S["sp_done"], HEADS_SG)
                evac(U_GB + m, d % 2, stage[:, m, :], ACT.Sigmoid, col("b_in", 40 + m)).then_inc(dense_free[d % 2], 1)
            act.wait_ge(S["unit_done"], U_SGO)
            for c in range(KC):
                high(ubuf[:, c, :], x_hi[:, c, 0:T], KC + c + 1)
            for m in range(8):
                tick(Part(U_SGO), m)
                if m == 2:
                    for c in range(KC):
                        act.wait_ge(S["yc_ready"], c + 1)
                        square(KC + c, sq[:, c % 2, :], y1[:, c, :])
                if m == 5:
                    root(2 * KC, rstd[:, :], pair[:, 0, :])
                    for c in range(KC):
                        act.wait_ge(S["t_ready"], c + 1)
                        act.activation(y1[:, c, :], y1[:, c, :], ACT.Silu, bias=col("conv_ln_b", c),
                                       scale=col("conv_ln_g", c)).then_inc(S["val_ready"], 1)
            act.wait_ge(S["unit_done"], U_CVO)
            for c in range(KC):
                high(y1[:, c, :], x_hi[:, c, 0:T], 2 * KC + c + 1)
            for m in range(8):
                tick(Part(U_CVO), m)
            act.wait_ge(S["unit_done"], U_OUT)
            for c in range(KC):
                high(gate_a[:, c, :], x_hi[:, c, 0:T], 3 * KC + c + 1)
            for m in range(9):
                if m < 8:
                    tick(Part(U_OUT), m)
                if m:
                    d = U_OUT - 8 + m - 1
                    act.wait_ge(dense_free[d % 2], d // 2 + 1)
                    square(2 * KC + m - 1, sq[:, (m - 1) % 2, :], y1[:, m - 1, :])
            barrier(act, 1)

            total_root(1, 3 * KC, rrs[:, :], pair[:, 0, :])
            for t in range(NT):
                act.wait_ge(S["tr_done"], t + 1)
                act.activation(htok[:, t, :], dense[t % 2][:, :, :].rearrange("p a b -> p (a b)"), ACT.Copy).then_inc(S["ht_ready"], 1)
                act.wait_ge(S["ht_ready"], t + 1)
                act.dma_start(hrows[t * P:(t + 1) * P, :], htok[:, t, :]).then_inc(S["hrows_in"], 16)
            act.wait_ge(S["gx_ready"], 1)
            act.activation(rt[:, 10, :, 0:GROUPS], rt[:, 10, :, 0:GROUPS], ACT.Exp).then_inc(S["ge_ready"], 1)
            act.wait_ge(S["gx_ready"], 2)
            act.activation(rs[:, 20, :], rs[:, 20, :], ACT.Exp).then_inc(S["ge_ready"], 1)

            def columns(e, par):
                act.wait_ge(S["xt_done"], e + 1)
                act.activation(xt_hi[:, par, :, :].rearrange("p c t -> p (c t)"),
                               pair[:, :, :].rearrange("p a b -> p (a b)"), ACT.Copy).then_inc(S["xth_done"], 1)

            def results(done, par, scattered):
                act.wait_ge(S["unit_done"], done)
                need(act, ys_out[par], scattered)
                act.activation(yb[:, par, :], dense[1][:, :, :].rearrange("p a b -> p (a b)"), ACT.Copy).then_inc(S["yb_ready"], 1)

            columns(0, 0)

            def expert(k, w, par, before):
                e = 2 * k + par
                j0 = PER_EXPERT * par
                for j in range(PER_EXPERT):
                    tick(w, j0 + j)
                    if j == 0 and before:
                        results(w.u + j0, 1 - par, 16 * (k - 1))
                    if j == 4:
                        act.wait_ge(S["unit_done"], w.u + j0 + 4)
                        need(act, S["u_free"], e + 1)
                        act.activation(gs[:, :], dense[0][:, 0, :], ACT.Silu).then_inc(S["silu_done"], 1)
                    if j == 5:
                        columns(e + 1, 1 - par)
                    if j == 11:
                        act.wait_ge(S["bat_done"], e + 2)
                        act.activation(at_hi[:, par, :, :].rearrange("p c t -> p (c t)"), duo[:, 0, :], ACT.Copy).then_inc(S["ath_done"], 1)

            for k in range(2):
                expert(k, MOE(k), 0, k > 0)
                expert(k, MOE(k), 1, True)
            with act.Fori(2, EXPERTS // 2) as k:
                expert(k, MOE(k), 0, True)
                expert(k, MOE(k), 1, True)
            tick(Part(U_LAST), 0)
            results(U_LAST, 1, 16 * (EXPERTS // 2 - 1))
            skip(Part(U_LAST), 1, 4)
            for j in range(5, 8):
                tick(Part(U_LAST), j)
                if j == 5:
                    results(U_LAST + 4, 0, 16 * (EXPERTS // 2 - 1))
            act.wait_ge(ys_out[0], 16 * EXPERTS // 2)
            extra = act.value_load(eint[0:1, EXTRA:EXTRA + 1])
            with act.Fori(0, EXTRA) as b:
                with act.If(extra > b):
                    e = act.value_load(eint[0:1, bass.ds(b, 1)], min_val=0, max_val=EXPERTS - 1)
                    for dst, u in ((bg, 0), (bu, 4), (bd, 2 * PER_EXPERT - 4)):
                        act.dma_start(dst[:, :, :], W[bass.ds(e * PER_EXPERT + U_MOE + u, 4)].rearrange("u p n -> p u n")
                                      ).then_inc(S["bw_in"], 16)
                    act.wait_ge(S["bx_done"], b + 1)
                    act.activation(bx[:, :, :].rearrange("p c t -> p (c t)"), pair[:, :, :].rearrange("p a b -> p (a b)"), ACT.Copy).then_inc(S["bx_ready"], 1)
                    act.wait_ge(S["bgu_done"], b + 1)
                    act.activation(gs[:, :], dense[0][:, 0, :], ACT.Silu).then_inc(S["bg_ready"], 1)
                    act.wait_ge(S["bs_done"], b + 1)
                    act.activation(ba[:, :, :].rearrange("p c t -> p (c t)"), duo[:, 0, :], ACT.Copy).then_inc(S["bat_ready"], 1)
                    act.wait_ge(S["bd_done"], b + 1)
                    act.activation(yb[:, 0, :], dense[1][:, :, :].rearrange("p a b -> p (a b)"), ACT.Copy).then_inc(S["by_ready"], 1)
            for t in range(NT):
                act.wait_ge(S["x2_ready"], t + 1)
                need(act, S["tsq_used"], t - 1)
                act.activation(tsq[:, t % 2, :, :], y1[:, :, t * P:(t + 1) * P], ACT.Square).then_inc(S["tsq_ready"], 1)
            act.wait_ge(S["tsq_used"], NT)
            act.activation(rrs[:, :], pair[:, 0, :], ACT.Sqrt, bias=consts[:, C_EPS:C_EPS + 1]).then_inc(S["root_ready"], 1)
            barrier(act, 2)

            def two(ap):
                return ap.rearrange("p (h t) -> p h t", h=2)

            with act.Fori(0, LAYERS) as l:
                w = LAYER(l)
                n0 = 3 * KC + l * SQS
                v0 = 4 * KC + l * VALS
                used = lambda d: 32 + l * USES + d // 2

                def root2(n, bank=pair):
                    act.wait_ge(S["sq_used"], n)
                    act.activation(two(rstd2[:, :]), bank[:, :, 0:HALF], ACT.Sqrt, bias=c2[:, D_EPS:D_EPS + 1]
                                   ).then_inc(S["root_ready"], 1)

                def copy_out(w, j, out, func=ACT.Copy):
                    act.wait_ge(S["unit_done"], w.u + j + 1)
                    act.activation(two(out), dense[j % 2][:, :, 0:HALF], func).then_inc(dense_free[j % 2], 1)

                for c in range(KC):
                    act.wait_ge(S["fr_done"], l * 8 + c + 2)
                    square(n0 + c, sq2[:, c % 2, :], res[:, c, :])
                root2(n0 + 8)
                for c in range(KC):
                    high(val2[:, c % 3, :], x_hi[:, c, :], v0 + c + 1)
                for j in range(5):
                    tick(w, j)
                    copy_out(w, j, qb[:, j, :] if j < 4 else kb[:, :])
                tick(w, 5)
                act.wait_ge(S["unit_done"], w.u + 6)
                act.activation(vb[0:META, 0, :], dense[1][0:META, 0, 0:P], ACT.Copy)
                act.activation(vb[:, 1:4, :], dense[1][:, 0, P:4 * P].rearrange("p (t c) -> p t c", t=3), ACT.Copy)
                act.activation(vb[:, 4, :], dense[1][:, 1, 0:P], ACT.Copy).then_inc(dense_free[1], 1)

                def weights_out(i, hp):
                    n, g, q0, nq, keys = item(i)
                    act.wait_ge(S["pt_done"], l * PTS + ptseq(i, hp) + 1)
                    if i:
                        need(act, S["pv_done"], l * 10 + i)
                    for kt, (_, _, nk) in enumerate(keys):
                        last = act.activation(pt[0:nk, i % 2, kt, 2 * hp:2 * hp + 2, 0:nq],
                                              pair[0:nk, 1, 2 * kt * P:(2 * kt + 2) * P].rearrange("p (h t) -> p h t", h=2)[:, :, 0:nq],
                                              ACT.Copy)
                    last.then_inc(S["pt_free"], 1)

                for s in range(STEPS):
                    if s < 12:
                        tick(w, 6 + s)
                    if 0 <= s - 1 < 10:
                        weights_out(s - 1, 0)
                    if s < 10:
                        n, g, q0, nq, keys = item(s)
                        nk = sum(x[2] for x in keys)
                        act.wait_ge(S["mk_ready"], l * 10 + s + 2)
                        for h in range(4):
                            row = sc[0:nq, s % 2, h, 0:nk]
                            act.activation(row, row, ACT.Exp, bias=sm[0:nq, s % 4, 1, h:h + 1], accum_out=sm[0:nq, s % 4, 3, h:h + 1])
                        act.activation(sm[0:nq, s % 4, 2, :], sm[0:nq, s % 4, 2, :], ACT.Exp).then_inc(S["ex_done"], 1)
                    if s < 8:
                        copy_out(w, 6 + s, (bb if s < 4 else cb)[:, s % 4, :])
                    if 0 <= s - 1 < 10:
                        weights_out(s - 1, 1)
                    if s >= 9:
                        if s < 13:
                            act.wait_ge(S["cv_ready"], l * 4 + s - 9 + 1)
                            square(n0 + 8 + s - 9, sq2[:, (s - 9) % 2, :], cb[:, s - 9, :])
                    if s >= 4 and s % 2 == 0:
                        n = (s - 4) // 2
                        nq = META if n == 0 else P
                        act.wait_ge(S["om_ready"], l * QB + n + 2)
                        act.activation(orr[0:nq, 1:2], orr[0:nq, 0:1], ACT.Sqrt, bias=c2[0:nq, D_EPS:D_EPS + 1], scale=1.0 / 512
                                       ).then_inc(S["os_ready"], 1)
                    if s == 12:
                        root2(n0 + 12, duo)
                act.wait_ge(S["unit_done"], w.u + L_OUT)
                for c in range(4):
                    high(cb[:, c, :], x_hi[:, 4 + c, :], v0 + 8 + c + 1)
                act.wait_ge(S["pt_free"], l * PTS + PTS + 1)
                for c in range(4):
                    high(yat[:, c, :], x_hi[:, c, :])
                for m in range(8):
                    j = L_OUT + m
                    tick(w, j)
                    act.wait_ge(S["unit_done"], w.u + j + 1)
                    square(n0 + 12 + m, two(sq2[:, m % 2, :]), dense[j % 2][:, :, 0:HALF])
                    act.activation(two(fb[:, m, :]), dense[j % 2][:, :, 0:HALF], ACT.Copy, scale=lcol("mix_post", m)
                                   ).then_inc(dense_free[j % 2], 1)
                act.wait_ge(S["total_done"], l * 2 + 2)
                root2(n0 + 20)
                act.wait_ge(S["unit_done"], w.u + L_MLP)
                for c in range(KC):
                    act.wait_ge(S["res_ready"], l * 8 + c + 1)
                    if c >= 3:
                        act.wait_ge(S["x_ready"], 32 + l * FEED + 16 + c - 2)
                    act.activation(val2[:, c % 3, :], res[:, c, :], ACT.Copy, scale=lcol("mlp_pre", c)).then_inc(S["val_ready"], 1)
                    high(val2[:, c % 3, :], x_hi[:, c, :], v0 + 12 + c + 1)
                    square(n0 + 20 + c, sq2[:, c % 2, :], res[:, c, :])
                root2(n0 + 28)
                def output(c):
                    act.wait_ge(dense_free[c % 2], used(48 + L_MLP + 8 + c) + 1)
                    square(n0 + 28 + c, sq2[:, c % 2, :], fb[:, c, :])
                    act.wait_ge(S["sq_ready"], n0 + 28 + c + 1)
                    act.activation(fb[:, c, :], fb[:, c, :], ACT.Copy, scale=lcol("mlp_post", c))

                def quarter(q, last=False):
                    wq = LAYER(l, q)
                    vq = v0 + 20 + q * 8

                    def hidden(m):
                        j = L_MLP + m
                        act.wait_ge(dense_free[j % 2], 32 + l * USES + q * 8 + j // 2 + 1)
                        act.wait_ge(S["x_ready"], 32 + l * FEED + 24 + q * 8 + m - 2)
                        act.activation(val2[:, m % 3, :], rl[:, m % 2, :], ACT.Square).then_inc(S["val_ready"], 1)
                        high(val2[:, m % 3, :], k_hi[:, m, :], vq + m + 1)

                    for m in range(8):
                        tick(wq, L_MLP + m)
                        if m:
                            if m == 1:
                                act.wait_ge(S["unit_done"], wq.u + L_MLP)
                            hidden(m - 1)
                    hidden(7)
                    for m in range(8):
                        tick(wq, L_MLP + 8 + m)
                        if last and m:
                            output(m - 1)

                with act.Fori(0, QUARTERS - 1) as q:
                    quarter(q)
                quarter(QUARTERS - 1, True)
                output(KC - 1)
                act.wait_ge(S["total_done"], l * 2 + 3)
                root2(n0 + 36)
                skip(w, L_DUMMY, AHEAD)
                for j in range(L_DUMMY + AHEAD, PER_LAYER):
                    tick(w, j)

        @block.vector
        def _(dve):
            dc = Count(dve, S["dve_chain"])
            for name in ("u_free", "rot_used", "kv_ready", "pt_free", "mk_ready", "at2_ready", "om_ready"):
                dve.engine_nop().then_inc(S[name], FROM[name])

            def step(ins):
                dc.add(ins)
                dc.wait()

            def tick(w, j):
                v = j + AHEAD
                dve.wait_ge(S["hi_done"], w.u + v + 1)
                dve.tensor_tensor(w_lo[:, v % SPLIT, :], raw[:, v % RAW, :], w_hi[:, v % SPLIT, :].bitcast(F32),
                                  ALU.subtract).then_inc(S["w_ready"], 1)

            def skip(w, j, n):
                dve.wait_ge(S["hi_done"], w.u + j + AHEAD + n)
                dve.drain().then_inc(S["w_ready"], n)

            def low_part(n, src, hi, lo):
                dve.wait_ge(S["xh_done"], n)
                dve.tensor_tensor(lo, src, hi.bitcast(F32), ALU.subtract).then_inc(S["x_ready"], 1)

            def inverse(k, r):
                dve.wait_ge(S["root_ready"], k)
                step(dve.reciprocal(r, r))

            def add_squares(n, c, acc, ring):
                if c:
                    dve.wait_ge(S["sq_ready"], n + c + 1)
                    if c > 1:
                        dve.wait_ge(S["sq_used"], n + c)
                    dve.tensor_tensor(acc, ring[:, 0, :] if c == 1 else acc, ring[:, c % 2, :], ALU.add
                                      ).then_inc(S["sq_used"], 2 if c == 1 else 1)

            def scaled(out, x, gain, r):
                return dve.scalar_tensor_tensor(out, x, gain, r, ALU.mult, ALU.mult)

            for j in range(-AHEAD, 0):
                tick(Part(0), j)
            dve.wait_ge(S["const_in"], 16)
            dve.wait_ge(S["par_in"], 16)
            inverse(1, rstd[:, :])

            def feed_normed(n0, vals, xs, gain, r, hi, lo, width):
                for c in range(KC + 1):
                    if c < KC:
                        if c >= 3:
                            dve.wait_ge(S["x_ready"], n0 + c - 2)
                        scaled(vals[:, c % 3, :], xs[:, c, :], gain(c), r).then_inc(S["val_ready"], 1)
                    if c:
                        low_part(n0 + c, vals[:, (c - 1) % 3, :], hi[:, c - 1, 0:width], lo[:, c - 1, 0:width])

            feed_normed(0, val, stage, lambda c: col("norm_mix_g", c), rstd[:, :], x_hi, x_lo, T)

            taps = [(c, k) for c0 in range(0, DVE_CONV, 2) for k in range(TAPS) for c in (c0, c0 + 1)]
            done = [0]

            def convolve(n):
                for c, k in taps[done[0]:done[0] + n]:
                    if done[0] >= 2:
                        dve.wait_ge(S["conv_done"], done[0] - 1)
                    wc = col("conv_w", c * TAPS + k)
                    if k == 0:
                        ins = dve.tensor_scalar(y1[:, c, :], apad[:, c, 0:T], wc, col("conv_b", c), ALU.mult, ALU.add)
                    else:
                        ins = dve.scalar_tensor_tensor(y1[:, c, :], apad[:, c, k:k + T], wc, y1[:, c, :], ALU.mult, ALU.add)
                    ins.then_inc(S["conv_done"], 1)
                    done[0] += 1

            def gated(u, d, out, bias, gate):
                dve.wait_ge(S["unit_done"], u + 1)
                return dve.scalar_tensor_tensor(out, dense[d % 2][:, 0, :], bias, gate, ALU.add, ALU.mult)

            for m in range(8):
                tick(Part(U_A2), m)
            dve.wait_ge(S["pool_chain"], 1)
            for m in range(8):
                tick(Part(U_A1), m)
                d = U_A1 + m
                dve.wait_ge(dense_free[m % 2], m // 2 + 1)
                gated(U_A1 + m, d, apad[:, m, PAD:], col("b_in", m), stage[:, m, :]).then_inc(dense_free[d % 2], 1)
                dve.wait_ge(dense_free[d % 2], d // 2 + 1)
                if m >= 2:
                    convolve(TAPS_PER_STEP)
            dve.wait_ge(S["aux_in"], 48)

            def v_bias(h):
                for t in range(NT):
                    bank = (dense[0], dense[1], pair, duo)[2 * h + t // 2][:, t % 2, :]
                    dve.tensor_tensor(vtok[:, t, h * 512:(h + 1) * 512], bank, bv_sb[:, h * 512:(h + 1) * 512], ALU.add
                                      ).then_inc(S["v_sum"], 1)

            def v_stats(h):
                for t in range(NT):
                    dve.wait_ge(S["v_gelu"], NT * h + t + 1)
                    dc.add(dve.bn_stats(vst[:, t, h, :], vtok[:, t, h * 512:(h + 1) * 512]))

            for j in range(8):
                tick(Part(U_V), j)
                if j == 3:
                    dve.wait_ge(S["unit_done"], U_V + 4)
                    v_bias(0)
                if j == 7:
                    dve.wait_ge(S["unit_done"], U_V + 8)
                    v_bias(1)
                convolve(TAPS_PER_STEP)
                if j == 5:
                    v_stats(0)
            for m in range(8):
                tick(Part(U_U), m)
                if m == 0:
                    v_stats(1)
                    dc.wait()
                    for t in range(NT):
                        dc.add(dve.bn_aggr(vmv[:, t, :], vst[:, t, :, :].rearrange("p a b -> p (a b)")))
                    dc.wait()
                    dve.engine_nop().then_inc(S["ms_ready"], 1)
                    inverse(2, vrs[:, :])
                    for t in range(NT):
                        dve.tensor_scalar(vtok[:, t, :], vtok[:, t, :], vmv[:, t, 0:1], vrs[:, t:t + 1],
                                          ALU.subtract, ALU.mult).then_inc(S["vn_ready"], 1)
                convolve(TAPS_PER_STEP)
            for m in range(8):
                tick(Part(U_GA), m)
                if m == 0:
                    dve.wait_ge(S["rows_done"], 1)
                    for h in range(HEADS_SG):
                        dc.add(dve.scalar_tensor_tensor(bs_sb[:, h, :], pair[:, h // 4, (h % 4) * P:(h % 4 + 1) * P],
                                                        col("sg_ln_b", h), bs_sb[:, h, :], ALU.mult, ALU.add))
                    dc.wait()
                convolve(TAPS_PER_STEP)
                dve.wait_ge(S["sp_done"], m + 1)
                dve.wait_ge(S["x_ready"], KC)
                if m >= 2:
                    dve.wait_ge(S["val_ready"], KC + m - 1)
                need(dve, dense_free[m % 2], (U_U - 8 + m) // 2 + 1)
                blocks = val[:, m % 2, :].rearrange("p (n q) -> p n q", n=NT)
                dve.scalar_tensor_tensor(blocks, duo[:, m % 2, :].rearrange("p (n q) -> p n q", n=NT), col("sg_ln_g", m),
                                         bs_sb[:, m, :].unsqueeze(1).broadcast_to([P, NT, P]), ALU.mult, ALU.add
                                         ).then_inc(S["sp_free"], 1)
                dve.wait_ge(S["sp_free"], m + 1)
                dve.tensor_tensor(ubuf[:, m, :], val[:, m % 2, :], ubuf[:, m, :], ALU.mult).then_inc(S["val_ready"], 1)
            for m in range(8):
                tick(Part(U_GB), m)
                convolve(TAPS_PER_STEP)
            convolve(len(taps))
            for c in range(KC):
                low_part(KC + c + 1, ubuf[:, c, :], x_hi[:, c, 0:T], x_lo[:, c, 0:T])
            for m in range(8):
                tick(Part(U_SGO), m)
                d = U_SGO - 8 + m
                if m == 2:
                    dve.wait_ge(S["s1_done"], KC)
                    step(dve.tensor_copy(mu[:, :], pair[:, 0, :]))
                    for c in range(KC):
                        dve.tensor_tensor(y1[:, c, :], y1[:, c, :], mu[:, :], ALU.subtract).then_inc(S["yc_ready"], 1)
                if m == 5:
                    inverse(3, rstd[:, :])
                    for c in range(KC):
                        dve.tensor_tensor(y1[:, c, :], y1[:, c, :], rstd[:, :], ALU.mult).then_inc(S["t_ready"], 1)
                need(dve, dense_free[m % 2], (U_GB - 8 + m) // 2 + 1)
                gated(U_SGO + m, d, stage[:, m, :], col("b_sg_out", m), stage[:, m, :]).then_inc(dense_free[d % 2], 1)
            for c in range(KC):
                low_part(2 * KC + c + 1, y1[:, c, :], x_hi[:, c, 0:T], x_lo[:, c, 0:T])
            for m in range(8):
                tick(Part(U_CVO), m)
                d = U_CVO - 8 + m
                gated(U_CVO + m, d, gate_a[:, m, :], col("b_conv_out", m), gate_a[:, m, :]).then_inc(dense_free[d % 2], 1)
                dve.wait_ge(dense_free[d % 2], d // 2 + 1)
                dve.tensor_tensor(gate_a[:, m, :], gate_a[:, m, :], stage[:, m, :], ALU.add).then_inc(S["val_ready"], 1)
            for c in range(KC):
                low_part(3 * KC + c + 1, gate_a[:, c, :], x_hi[:, c, 0:T], x_lo[:, c, 0:T])
            dve.wait_ge(S["xr_in"], 16)
            for m in range(8):
                tick(Part(U_OUT), m)
                d = U_OUT - 8 + m
                if m:
                    add_squares(2 * KC, m - 1, mu[:, :], sq)
                dve.wait_ge(S["unit_done"], U_OUT + m + 1)
                dve.scalar_tensor_tensor(y1[:, m, :], dense[d % 2][:, 0, :], col("b_out", m), xr[:, m, :], ALU.add, ALU.add
                                         ).then_inc(dense_free[d % 2], 1)
            add_squares(2 * KC, KC - 1, mu[:, :], sq)
            barrier(dve, 1)

            dve.memset(at_hi[:, 1, :, :].bitcast(F32), 0.0)
            dve.memset(at_lo[:, 1, :, :].bitcast(F32), 0.0).then_inc(S["at_ready"], 1)
            inverse(4, rrs[:, :])
            for c in range(KC):
                scaled(hb[:, c, :], y1[:, c, :], col("norm_ffn_g", c), rrs[:, :]).then_inc(S["hb_ready"], 1)
            tt, ts, stt, red = dve.tensor_tensor, dve.tensor_scalar, dve.scalar_tensor_tensor, dve.tensor_reduce
            R = lambda i: rs[:, i, :]
            iota = lambda n: consts[:, C_IOTA:C_IOTA + n]
            wide = lambda ap, n: ap.unsqueeze(2).broadcast_to([P, NT, n])
            over = lambda ap, n: ap.unsqueeze(1).broadcast_to([P, NT, n])
            G, E = lg[:, :, 0:GROUPS], lg[:, :, GROUPS:ROUTER]

            def first_max(x, n, best, index):
                step(red(R(best), x, AX_X, ALU.max))
                step(tt(rt[:, 0, :, 0:n], x, wide(R(best), n), ALU.is_equal))
                step(stt(rt[:, 1, :, 0:n], rt[:, 0, :, 0:n], -64.0, over(iota(n), n), ALU.mult, ALU.add))
                step(red(R(index), rt[:, 1, :, 0:n], AX_X, ALU.min))
                step(ts(R(index), R(index), 64.0, None, ALU.add))

            dve.wait_ge(S["lg_done"], 1)
            dve.tensor_copy(lgT[0:ROUTER, :], duo[0:ROUTER, 0, :]).then_inc(S["lgt_ready"], 1)
            dve.wait_ge(S["lg_done"], 2)
            dve.wait_ge(S["mask_in"], 32)
            step(tt(lg[:, :, :], duo[:, 1, 0:NT * ROUTER].rearrange("p (t r) -> p t r", t=NT), over(rb_sb[:, :], ROUTER), ALU.add))
            first_max(G, GROUPS, 0, 1)
            tt(rt[:, 10, :, 0:GROUPS], G, wide(R(0), GROUPS), ALU.subtract).then_inc(S["gx_ready"], 1)
            step(tt(rt[:, 4, :, 0:GROUPS], over(iota(GROUPS), GROUPS), wide(R(1), GROUPS), ALU.is_equal))
            spread = rt[:, 0, :, :].rearrange("p t (g e) -> p t g e", g=GROUPS)
            step(tt(spread, E.rearrange("p t (g e) -> p t g e", g=GROUPS),
                    rt[:, 4, :, 0:GROUPS].unsqueeze(3).broadcast_to([P, NT, GROUPS, PER_GROUP]), ALU.mult))
            step(red(rt[:, 5, :, 0:PER_GROUP], spread.rearrange("p t g e -> p t e g"), AX_X, ALU.add))
            el = rt[:, 5, :, 0:PER_GROUP]
            first_max(el, PER_GROUP, 4, 5)
            step(tt(rt[:, 1, :, 0:PER_GROUP], over(iota(PER_GROUP), PER_GROUP), wide(R(5), PER_GROUP), ALU.is_equal))
            step(stt(rt[:, 11, :, 0:PER_GROUP], rt[:, 1, :, 0:PER_GROUP], -3.0e38, el, ALU.mult, ALU.add))
            first_max(rt[:, 11, :, 0:PER_GROUP], PER_GROUP, 6, 7)
            tt(R(20), R(6), R(4), ALU.subtract).then_inc(S["gx_ready"], 1)
            for j in range(2):
                step(stt(R(8 + j), R(1), float(PER_GROUP), R(5 + 2 * j), ALU.mult, ALU.add))
                step(tt(rt[:, 2 + j, :, :], over(iota(EXPERTS), EXPERTS), wide(R(8 + j), EXPERTS), ALU.is_equal))
            tt(rt[:, 6, :, :], rt[:, 2, :, :], rt[:, 3, :, :], ALU.add).then_inc(S["rank_ready"], 1)
            dve.wait_ge(S["rank_done"], 1)
            step(dve.tensor_copy(rt[:, 7, :, :], duo[:, 1, 0:NT * EXPERTS].rearrange("p (t e) -> p t e", t=NT)))
            step(dve.tensor_copy(rt[:, 8, 0, :], duo[:, 1, NT * EXPERTS:(NT + 1) * EXPERTS]))
            counts, more, pa, pb = rt[:, 8, 0, :], rt[:, 8, 1, :], rt[:, 9, 0, :], rt[:, 9, 1, :]
            step(ts(more, counts, float(P), None, ALU.is_gt))
            for k in (2, 3):
                step(stt(more, counts, float(k * P), more, ALU.is_gt, ALU.add))
            step(dve.tensor_copy(pa, more))
            for sh in (1, 2, 4, 8, 16):
                step(dve.tensor_copy(pb[:, 0:sh], pa[:, 0:sh]))
                step(tt(pb[:, sh:], pa[:, sh:], pa[:, 0:EXPERTS - sh], ALU.add))
                pa, pb = pb, pa
            before = rt[:, 9, 2, :]
            step(tt(before, pa, more, ALU.subtract))
            for j in range(2):
                step(tt(rt[:, 0, :, :], rt[:, 7, :, :], rt[:, 2 + j, :, :], ALU.mult))
                step(red(R(10 + j), rt[:, 0, :, :], AX_X, ALU.add))
                step(tt(rt[:, 0, :, :], rt[:, 2 + j, :, :], over(before, EXPERTS), ALU.mult))
                step(red(R(12 + j), rt[:, 0, :, :], AX_X, ALU.add))
                step(ts(R(14 + j), R(10 + j), float(P), None, ALU.is_ge))
                for k in (2, 3):
                    step(stt(R(14 + j), R(10 + j), float(k * P), R(14 + j), ALU.is_ge, ALU.add))
                step(stt(R(16 + j), R(14 + j), -float(P), R(10 + j), ALU.mult, ALU.add))
                step(tt(R(23), R(12 + j), R(14 + j), ALU.add))
                step(stt(R(24), R(23), float(EXPERTS - 1), R(8 + j), ALU.add, ALU.subtract))
                step(stt(R(25), R(14 + j), 0.0, R(24), ALU.is_gt, ALU.mult))
                step(tt(R(18 + j), R(8 + j), R(25), ALU.add))
            for k in range(2 * NT):
                j, t = k // NT, k % NT
                need(dve, S["list_done"], k - 1)
                row, blk = rs[:, 16 + j, t:t + 1], rs[:, 18 + j, t:t + 1]
                ts(onr[:, k % 2, :], iota(P), row, None, ALU.is_equal)
                ts(onb[:, k % 2, 0:BLOCKS], iota(BLOCKS), blk, consts[:, C_GTOK + k:C_GTOK + k + 1], ALU.is_equal, ALU.mult)
                ts(onb[:, k % 2, BLOCKS:], iota(BLOCKS), blk, consts[:, C_STOK + k:C_STOK + k + 1], ALU.is_equal, ALU.mult
                   ).then_inc(S["list_ready"], 1)
            dve.wait_ge(S["list_done"], 2 * NT)
            ts(idx[:, :], duo[:, 0, 0:2 * BLOCKS], float(UNUSED), None, ALU.add).then_inc(S["idx_ready"], 1)
            dve.wait_ge(S["ge_ready"], 2)
            step(red(R(2), rt[:, 10, :, 0:GROUPS], AX_X, ALU.add))
            step(dve.reciprocal(R(3), R(2)))
            step(ts(R(21), R(20), 1.0, None, ALU.add))
            step(dve.reciprocal(R(22), R(21)))
            step(tt(wts[:, 0, :], R(22), R(3), ALU.mult))
            step(tt(wts[:, 1, :], wts[:, 0, :], R(20), ALU.mult))
            cmp = rt[:, 0:2, :, :].rearrange("p a t e -> p (a t) e")[:, 0:EXTRA, :]
            step(tt(cmp, pa.unsqueeze(1).broadcast_to([P, EXTRA, EXPERTS]),
                    iota(EXTRA).unsqueeze(2).broadcast_to([P, EXTRA, EXPERTS]), ALU.is_le))
            step(red(rt[:, 8, 2, 0:EXTRA], cmp, AX_X, ALU.add))
            step(dve.tensor_copy(rt[:, 8, 2, EXTRA:EXTRA + 1], pa[:, EXPERTS - 1:EXPERTS]))
            step(dve.tensor_copy(eint[:, :], rt[:, 8, 2, 0:EXTRA + 1]))

            def columns(e, par):
                dve.wait_ge(S["xth_done"], e + 1)
                tt(xt_lo[:, par, :, :].rearrange("p c t -> p (c t)"), pair[:, :, :].rearrange("p a b -> p (a b)"),
                   xt_hi[:, par, :, :].rearrange("p c t -> p (c t)").bitcast(F32), ALU.subtract).then_inc(S["xt_ready"], 1)

            columns(0, 0)
            with dve.Fori(0, EXPERTS // 2) as k:
                w = MOE(k)
                for par in range(2):
                    e = 2 * k + par
                    j0 = PER_EXPERT * par
                    for j in range(PER_EXPERT):
                        if j != 8:
                            tick(w, j0 + j)
                        if j == 6:
                            columns(e + 1, 1 - par)
                        if j == 8:
                            dve.wait_ge(S["unit_done"], w.u + j0 + 8)
                            dve.wait_ge(S["silu_done"], e + 2)
                            dve.wait_ge(S["bat_done"], e + 1)
                            tt(ab[:, :], dense[0][:, 1, :], gs[:, :], ALU.mult).then_inc(S["u_free"], 1)
                            tick(w, j0 + j)
                        if j == 11:
                            dve.wait_ge(S["ath_done"], e + 1)
                            tt(at_lo[:, par, :, :].rearrange("p c t -> p (c t)"), duo[:, 0, :],
                               at_hi[:, par, :, :].rearrange("p c t -> p (c t)").bitcast(F32), ALU.subtract).then_inc(S["at_ready"], 1)
            tick(Part(U_LAST), 0)
            skip(Part(U_LAST), 1, 4)
            for j in range(5, 8):
                tick(Part(U_LAST), j)
            extra = dve.value_load(eint[0:1, EXTRA:EXTRA + 1])
            with dve.Fori(0, EXTRA) as b:
                with dve.If(extra > b):
                    dve.wait_ge(S["bg_ready"], b + 1)
                    tt(ab[:, :], dense[0][:, 1, :], gs[:, :], ALU.mult).then_inc(S["ba_ready"], 1)

            def back(t):
                dve.wait_ge(S["o2_done"], t + 1)
                tok = y1[:, :, t * P:(t + 1) * P]
                tt(tok, dense[t % 2][:, :, :].rearrange("p a (c t) -> p (a c) t", t=P), tok, ALU.add).then_inc(S["x2_ready"], 1)

            for t in range(NT):
                dve.wait_ge(y2_in[t % 2], 16 * (t // 2 + 1))
                need(dve, S["o2_done"], t - 1)
                step(ts(ot2[:, t % 2, :], y2b[:, t % 2, 0, :], wts[:, 0, t:t + 1], None, ALU.mult))
                stt(ot2[:, t % 2, :], y2b[:, t % 2, 1, :], wts[:, 1, t:t + 1], ot2[:, t % 2, :], ALU.mult, ALU.add
                    ).then_inc(S["o2_ready"], 1)
                if t:
                    back(t - 1)
            back(NT - 1)
            dve.wait_ge(S["meta_in"], 32)
            step(dve.tensor_copy(res[:, :, 0:META], meta_sb[:, :, :]))
            barrier(dve, 2)
            inverse(5, rrs[:, :])
            for c in range(KC):
                scaled(res[:, c, META:], y1[:, c, :], col("norm_final_g", c), rrs[:, :]
                       ).then_inc(S["fr_done"], 1 if c else FROM["fr_done"] - KC + 1)

            def two(ap):
                return ap.rearrange("p (h t) -> p h t", h=2)

            with dve.Fori(0, LAYERS) as l:
                dc.loop(l, 0, CHAIN)
                w = LAYER(l)
                n0 = 3 * KC + l * SQS
                x0 = 32 + l * FEED
                used = lambda d: 32 + l * USES + d // 2
                halves_of = lambda: pair[:, :, 0:HALF]

                def rms(k, ready=None, count=None):
                    if ready is None:
                        inverse(5 + l * 5 + k, rstd2[:, :])
                    else:
                        dve.wait_ge(S["root_ready"], 5 + l * 5 + k)
                        dve.reciprocal(rstd2[:, :], rstd2[:, :]).then_inc(ready, 1)
                        dve.wait_ge(ready, count)

                rms(1)
                dve.wait_ge(S["lpar_in"], l * 16 + 16)
                feed_normed(x0, val2, res, lambda c: lcol("mix_pre", c), rstd2[:, :], x_hi, x_lo, L)
                for j in range(5):
                    tick(w, j)
                    q = qb[:, j, :] if j < 4 else kb[:, :]
                    dve.wait_ge(S["rot_done"], l * 5 + j + 1)
                    need(dve, S["kv_ready"], l * 5 + j + 1)
                    dve.tensor_tensor(two(rot[:, :]), halves_of(), two(c2[:, D_SIN:D_SIN + L]), ALU.mult).then_inc(S["rot_used"], 1)
                    step(dve.tensor_tensor(q, q, c2[:, D_COS:D_COS + L], ALU.mult))
                    dve.wait_ge(S["rot_used"], l * 5 + j + 2)
                    dve.tensor_tensor(q, q, rot[:, :], ALU.add).then_inc(S["kv_ready"], 1)
                tick(w, 5)
                dve.wait_ge(S["pad_ready"], l + 1)
                for s in range(STEPS):
                    if s >= 5 and s % 2 == 1:
                        n = (s - 5) // 2
                        q0, nq = (0, META) if n == 0 else (META + P * (n - 1), P)
                        dve.wait_ge(S["os_ready"], l * QB + n + 1)
                        step(dve.reciprocal(orr[0:nq, 2:3], orr[0:nq, 1:2]))
                        o = ot[0:nq, n % 2, :, :].rearrange("p h d -> p (h d)")
                        dve.tensor_scalar(o, o, orr[0:nq, 2:3], None, ALU.mult).then_inc(S["o_ready"], 1)
                    if s < 10:
                        n, g, q0, nq, keys = item(s)
                        nk = sum(x[2] for x in keys)
                        dve.wait_ge(S["sc_done"], l * 10 + s + 1)
                        if s >= 2:
                            dve.wait_ge(S["pt_done"], l * PTS + ptseq(s - 2, 1) + 1)
                        mk = D_MASK[min(n, 2)]
                        x = sc[0:nq, s % 2, :, 0:nk]
                        M = lambda i: sm[0:nq, s % 4, i, :]
                        step(dve.scalar_tensor_tensor(x, duo[0:nq, :, :].rearrange("p a (b k) -> p (a b) k", b=2)[:, :, 0:nk], HD ** -0.5,
                                                      c2[0:nq, mk:mk + nk].unsqueeze(1).broadcast_to([nq, 4, nk]), ALU.mult, ALU.add))
                        step(dve.tensor_reduce(M(0), x, AX_X, ALU.max))
                        sinks = lcol("sinks", 4 * g, 4)[0:nq]
                        step(dve.tensor_tensor(M(0), M(0), sinks, ALU.max))
                        step(dve.tensor_scalar(M(1), M(0), -1.0, None, ALU.mult))
                        dve.tensor_tensor(M(2), sinks, M(0), ALU.subtract).then_inc(S["mk_ready"], 1)
                    if s < 12:
                        tick(w, 6 + s)
                    if 0 <= s - 3 < 10:
                        i = s - 3
                        n, g, q0, nq, keys = item(i)
                        M = lambda k: sm[0:nq, i % 4, k, :]
                        dve.wait_ge(S["pv_done"], l * 10 + i + 2)
                        if n >= 2 and g == 0:
                            dve.wait_ge(S["pt_done"], l * PTS + atseq(n - 2) + 1)
                        step(dve.tensor_tensor(M(4), M(3), M(2), ALU.add))
                        step(dve.reciprocal(M(5), M(4)))
                        dve.tensor_tensor(ot[0:nq, n % 2, 4 * g:4 * g + 4, :], pair[0:nq, 0, 0:4 * HD].rearrange("p (h d) -> p h d", h=4),
                                          M(5).unsqueeze(2).broadcast_to([nq, 4, HD]), ALU.mult).then_inc(S["at2_ready"], 1)
                        if g == 1:
                            dve.wait_ge(S["at2_ready"], l * 10 + i + 2)
                            o = ot[0:nq, n % 2, :, :].rearrange("p h d -> p (h d)")
                            need(dve, S["om_ready"], l * QB + n + 1)
                            dve.scalar_tensor_tensor(rot[0:nq, 0:512], o, 1.0, o, ALU.mult, ALU.mult, accum_out=orr[0:nq, 0:1]
                                                     ).then_inc(S["om_ready"], 1)
                    if s == STEPS - 1:
                        rms(2)
                        for c in range(4):
                            scaled(cb[:, c, :], cb[:, c, :], lcol("conv_g", c), rstd2[:, :]).then_inc(S["val_ready"], 1)
                    if s >= 5 and s % 2 == 1:
                        n = (s - 5) // 2
                        dve.wait_ge(S["pt_done"], l * PTS + atseq(n) + 1)
                        q0, nq = (0, META) if n == 0 else (META + P * (n - 1), P)
                        dve.tensor_tensor(yat[:, :, q0:q0 + nq], pair[:, 1, :].rearrange("p (c t) -> p c t", c=4)[:, :, 0:nq],
                                          lcol("attn_g", 0, 4).unsqueeze(2).broadcast_to([P, 4, nq]), ALU.mult).then_inc(S["pt_free"], 1)
                    if 8 <= s < 12:
                        m, j = s - 8, 6 + s
                        dve.wait_ge(S["unit_done"], w.u + j + 1)
                        dve.wait_ge(dense_free[(j - 4) % 2], used(j - 4) + 1)
                        dve.tensor_tensor(two(up[:, m, 2:]), dense[j % 2][:, :, 0:HALF], two(cb[:, m, :]), ALU.mult).then_inc(dense_free[j % 2], 1)
                        dve.wait_ge(dense_free[j % 2], used(j) + 1)
                        step(dve.tensor_scalar(cb[:, m, :], up[:, m, 0:L], lcol("conv_w", m * 3), None, ALU.mult))
                        for k in (1, 2):
                            step(dve.scalar_tensor_tensor(cb[:, m, :], up[:, m, k:k + L], lcol("conv_w", m * 3 + k), cb[:, m, :],
                                                          ALU.mult, ALU.add))
                        dve.tensor_tensor(cb[:, m, :], cb[:, m, :], bb[:, m, :], ALU.mult).then_inc(S["cv_ready"], 1)
                for i, c in enumerate((4, 5, 6, 7, 0, 1, 2, 3)):
                    src = yat[:, c, :] if c < 4 else cb[:, c - 4, :]
                    low_part(x0 + 8 + i + 1, src, x_hi[:, c, :], x_lo[:, c, :])
                for m in range(8):
                    tick(w, L_OUT + m)
                    if m:
                        add_squares(n0 + 12, m - 1, acc[:, :], sq2)
                add_squares(n0 + 12, KC - 1, acc[:, :], sq2)

                rms(3, S["inv_ready"], l * 2 + 1)
                for c in range(KC + 1):
                    if c < KC:
                        dve.wait_ge(S["fs_ready"], l * 16 + c + 1)
                        dve.tensor_tensor(res[:, c, :], res[:, c, :], fb[:, c, :], ALU.add).then_inc(S["res_ready"], 1)
                    if c:
                        low_part(x0 + 16 + c, val2[:, (c - 1) % 3, :], x_hi[:, c - 1, :], x_lo[:, c - 1, :])
                dve.wait_ge(S["root_ready"], 5 + l * 5 + 4)
                dc.add(dve.reciprocal(rstd2[:, :], rstd2[:, :]))
                def quarter(q, last=False):
                    wq = LAYER(l, q)
                    xq = x0 + 24 + q * 8
                    for m in range(9):
                        if m:
                            j = L_MLP + m - 1
                            dve.wait_ge(S["unit_done"], wq.u + j + 1)
                            if m == 1:
                                dc.wait()
                            dve.scalar_tensor_tensor(two(rl[:, (m - 1) % 2, :]), dense[j % 2][:, :, 0:HALF], 0.0, two(rstd2[:, :]),
                                                     ALU.max, ALU.mult).then_inc(dense_free[j % 2], 1)
                        tick(wq, L_MLP + m)
                        if m:
                            low_part(xq + m, val2[:, (m - 1) % 3, :], k_hi[:, m - 1, :], k_lo[:, m - 1, :])
                    for m in range(8):
                        if m:
                            tick(wq, L_MLP + 8 + m)
                        j = L_MLP + 8 + m
                        if last and m:
                            add_squares(n0 + 28, m - 1, acc[:, :], sq2)
                        dve.wait_ge(S["unit_done"], wq.u + j + 1)
                        if m == 0:
                            dve.wait_ge(S["fb_zero"], l + 1)
                        dve.wait_ge(dense_free[j % 2], 32 + l * USES + q * 8 + j // 2 - 7)
                        dve.tensor_tensor(two(fb[:, m, :]), dense[j % 2][:, :, 0:HALF], two(fb[:, m, :]), ALU.add
                                          ).then_inc(dense_free[j % 2], 1)

                with dve.Fori(0, QUARTERS - 1) as q:
                    quarter(q)
                quarter(QUARTERS - 1, True)
                add_squares(n0 + 28, KC - 1, acc[:, :], sq2)
                rms(5, S["inv_ready"], l * 2 + 2)
                for c in range(KC):
                    dve.wait_ge(S["fs_ready"], l * 16 + 8 + c + 1)
                    dve.tensor_tensor(res[:, c, :], res[:, c, :], fb[:, c, :], ALU.add).then_inc(S["fr_done"], 1)
                skip(w, L_DUMMY, AHEAD)
                for j in range(L_DUMMY + AHEAD, PER_LAYER):
                    tick(w, j)
                dc.end(LAYERS)


def channels(v):
    return v.reshape(-1, P).T


def k_chunks(w):
    return w.reshape(-1, P, w.shape[-1])


def dense_units(w):
    n = w.shape[-1] // P
    return k_chunks(w).reshape(KC, P, n, P).transpose(2, 1, 0, 3).reshape(n, P, UNIT)


def half_units(w):
    return k_chunks(w).reshape(4, 2, P, 512).transpose(0, 2, 1, 3).reshape(4, P, UNIT)


def weight_stream(i):
    W = np.zeros((UNITS, P, UNIT), np.float32)
    w_in = i["w_in"][0]
    for u, c in ((U_A2, D), (U_A1, 0), (U_U, 2 * D), (U_GA, 4 * D), (U_GB, 5 * D)):
        W[u:u + 8] = dense_units(w_in[:, c:c + D])
    for h in range(2):
        W[U_V + 4 * h:U_V + 4 * h + 4] = half_units(w_in[:, 3 * D + h * 512:3 * D + (h + 1) * 512])
    for u, name in ((U_SGO, "w_sg_out"), (U_CVO, "w_conv_out"), (U_OUT, "w_out")):
        W[u:u + 8] = dense_units(i[name][0])
    for e in range(EXPERTS):
        u = U_MOE + e * PER_EXPERT
        W[u:u + 4] = half_units(i["w_expert_gate"][0, e])
        W[u + 4:u + 8] = half_units(i["w_expert_up"][0, e])
        d = u + PER_EXPERT + 8 if e < EXPERTS - 1 else U_LAST
        W[d:d + 4] = k_chunks(i["w_expert_down"][0, e])
    for l in range(LAYERS):
        u = U_LAYER + l * PER_LAYER
        w_in = i["w_in_2"][l]
        heads = w_in[:, 0:512].reshape(D, 2, 4, HD).transpose(0, 2, 1, 3).reshape(D, 512)
        W[u:u + 4] = dense_units(heads)
        W[u + 4:u + L_OUT] = dense_units(w_in[:, 512:])
        W[u + L_OUT:u + L_MLP] = dense_units(i["w_out_2"][l])
        for q in range(QUARTERS):
            m = u + L_MLP + 16 * q
            W[m:m + 8] = dense_units(i["w_up_2"][l][:, q * D:(q + 1) * D])
            W[m + 8:m + 16] = dense_units(i["w_down_2"][l][q * D:(q + 1) * D])
    return W


def everywhere(a):
    return np.broadcast_to(a, (P,) + a.shape)


def parameters(i):
    par = np.zeros((P, NPAR), np.float32)
    for name in COLS:
        v = i[name]
        if name == "conv_w":
            v = v[0].reshape(TAPS, KC, P).transpose(2, 1, 0).reshape(P, KC * TAPS)
        else:
            v = channels(v.reshape(-1))
        par[:, COLS[name]:COLS[name] + v.shape[1]] = v
    lpar = np.zeros((LAYERS, P, NLPAR), np.float32)
    for l in range(LAYERS):
        for name, v in (("mix_pre", channels(i["mix_pre_g_2"][l])), ("attn_g", channels(i["attn_out_g_2"][l])),
                        ("conv_g", channels(i["conv_out_g_2"][l])), ("mix_post", channels(i["mix_post_g_2"][l])),
                        ("mlp_pre", channels(i["mlp_pre_g_2"][l])), ("mlp_post", channels(i["mlp_post_g_2"][l])),
                        ("conv_w", i["conv_w_2"][l].reshape(3, AC, P).transpose(2, 1, 0).reshape(P, 12)),
                        ("sinks", everywhere(i["sinks_2"][l]))):
            lpar[l][:, LCOLS[name]:LCOLS[name] + v.shape[1]] = v
    return par, lpar


def constants():
    p = np.arange(P)
    cst = np.zeros((P, NCONST), np.float32)
    cst[:, C_IDENT:C_IDENT + P] = np.eye(P)
    cst[:, C_BEFORE:C_BEFORE + P] = p[:, None] < p[None, :]
    cst[:, C_ONE:C_ONE + P] = 1
    cst[:, C_MEAN:C_MEAN + P] = 1 / D
    cst[:, C_IOTA:C_IOTA + P] = p
    cst[:, C_EPS] = EPS
    for j in range(2):
        for t in range(NT):
            cst[:, C_GTOK + j * NT + t] = t * P + p - UNUSED
            cst[:, C_STOK + j * NT + t] = 2 * (t * P + p) + j - UNUSED
    c2 = np.zeros((P, NCONST2), np.float32)
    c2[:, D_MEAN:D_MEAN + P] = 1 / D
    c2[:, D_MEAN2:D_MEAN2 + P] = 2 / D
    c2[:, D_IDENT:D_IDENT + P] = np.eye(P)
    c2[:, D_EPS] = EPS
    rot = HD // 8
    freq = np.power(np.float32(500000.0), -np.arange(0, 2 * rot, 2, dtype=np.float32) / np.float32(2 * rot)).astype(np.float32)
    c2[:, D_COS:D_COS + L] = 1
    for h in range(0, P, HD):
        for d in range(rot):
            c2[h + rot + d, D_ROT + h + d] = -1
            c2[h + d, D_ROT + h + rot + d] = 1
            ang = (np.arange(L, dtype=np.float32) * freq[d]).astype(np.float32)
            for r in (h + d, h + rot + d):
                c2[r, D_COS:D_COS + L] = np.cos(ang)
                c2[r, D_SIN:D_SIN + L] = np.sin(ang)
    q = p[:, None]
    j = np.arange(META)[None]
    c2[:, D_MASK[0]:D_MASK[0] + META] = np.where(j <= q, 0, MASKED)
    j = np.arange(META + P)[None]
    c2[:, D_MASK[1]:D_MASK[1] + META + P] = np.where((j <= META + q) & (j > META + q - P), 0, MASKED)
    j = np.arange(2 * P)[None]
    c2[:, D_MASK[2]:D_MASK[2] + 2 * P] = np.where((j > q) & (j <= q + P), 0, MASKED)
    return cst, c2


def kernel(**inputs):
    import concourse.bacc as bacc
    from concourse.bass_utils import run_bass_kernel_spmd

    i = {k: np.asarray(v) for k, v in inputs.items()}
    par, lpar = parameters(i)
    cst, c2 = constants()
    router = np.concatenate([i["w_router_group"][0], i["w_router_expert"][0]], axis=1)
    arrays = {
        "W": weight_stream(i),
        "xT": i["x"][0].reshape(T, KC, P).transpose(2, 1, 0),
        "par": par, "lpar": lpar, "cst": cst, "cst2": c2,
        "bv": everywhere(i["b_in"][0, 3 * D:4 * D]),
        "bs": everywhere(i["b_sg"][0]),
        "wsT": i["w_sg"][0].transpose(2, 0, 1),
        "wr": k_chunks(router).transpose(1, 0, 2),
        "rb": everywhere(np.concatenate([i["b_router_group"][0], i["b_router_expert"][0]])),
        "metaT": i["meta_tokens_2"].reshape(META, KC, P).transpose(2, 1, 0),
    }
    nc = bacc.Bacc("TRN2", target_bir_lowering=False, num_devices=1)
    args, given = {}, {}
    for name, a in arrays.items():
        a = np.ascontiguousarray(a)
        given[f"in_{name}_dram"] = a
        args[name] = nc.dram_tensor(f"in_{name}_dram", a.shape, mybir.dt.from_np(a.dtype), kind="ExternalInput").ap()
    args["out"] = nc.dram_tensor("out_dram", (P, KC, T), F32, kind="ExternalOutput").ap()
    program(nc, **args)
    r = run_bass_kernel_spmd(nc, [given], core_ids=[0])
    got = r.results[0]["out_dram"]
    return np.ascontiguousarray(got.transpose(2, 1, 0).reshape(1, T, D))
```
